# Optimizing a Trainium2 kernel written in Bass

```python
import math
import jax
import jax.numpy as jnp
from jax import lax
import numpy as np

D_MODEL = 1024
BATCH = 1
SEQ = 128
DEPTH = 2
DEC_BATCH = 1
DEC_SEQ = 512
PAST_LEN = 128

GRID_W = 64
N_SSM_LAYERS = (DEPTH + 1) // 2
N_ATTN_LAYERS = DEPTH // 2
EPS = 1e-6
F_FLOOR = 1e-30
SSD_D_INNER = D_MODEL
SSD_HEAD_DIM = 64
SSD_HEADS = SSD_D_INNER // SSD_HEAD_DIM
SSD_GROUPS = 2
SSD_HPG = SSD_HEADS // SSD_GROUPS
SSD_STATE = 128
SSD_XBC = SSD_D_INNER + 2 * SSD_GROUPS * SSD_STATE
SSD_CONV = 3
SSD_CHUNK = 128
HG_D = D_MODEL
HG_HEAD_DIM = 128
HG_HEADS = HG_D // HG_HEAD_DIM
HG_CHUNK = 32
SSM_IN = SSD_D_INNER + SSD_XBC + 2 * SSD_HEADS + 5 * HG_D
ATTN_HEADS = 16
ATTN_KV_HEADS = 4
ATTN_GROUP = ATTN_HEADS // ATTN_KV_HEADS
ATTN_HEAD_DIM = D_MODEL // ATTN_HEADS
ATTN_IN = (ATTN_HEADS + 2 * ATTN_KV_HEADS) * ATTN_HEAD_DIM
ATTN_BLOCK = 128
ROPE_THETA = 10000.0
FFN_DIM = 2816
FFN_CONV = 3

kernel_name = 'hybrid_ssd_hgrn2_gqa_diffusion_step'

def rms_norm(x, g):
    xf = x.astype(jnp.float32)
    y = xf * lax.rsqrt(jnp.mean(xf * xf, axis=-1, keepdims=True) + EPS)
    return (y * g.astype(jnp.float32)).astype(x.dtype)

def dwconv(x, w, b):
    y = lax.conv_general_dilated(x, w[:, None, :].astype(x.dtype), window_strides=(1,), padding='SAME',
                                 dimension_numbers=('NWC', 'WIO', 'NWC'), feature_group_count=x.shape[-1])
    return y + b.astype(x.dtype)

def adaln(x, g, shift, scale):
    return rms_norm(x, g) * (1.0 + scale) + shift

def gated_residual(x, y, g, gate):
    return x + gate * rms_norm(y, g)

def modulation(cond, w, b):
    return jnp.split(jax.nn.silu(cond) @ w + b, 6, axis=-1)

def segsum_exp(a):
    T = a.shape[-1]
    xa = jnp.broadcast_to(a[..., :, None], a.shape + (T,))
    strict = jnp.tril(jnp.ones((T, T), dtype=bool), -1)
    tri = jnp.tril(jnp.ones((T, T), dtype=bool))
    cs = jnp.cumsum(jnp.where(strict, xa, 0.0), axis=-2)
    return jnp.where(tri, jnp.exp(jnp.where(tri, cs, 0.0)), 0.0)

def ssd_chunked(xd, a_dt, bm, cm, s0):
    b, L, g, r, p = xd.shape
    n = bm.shape[-1]
    nc = L // SSD_CHUNK
    X = xd.reshape(b, nc, SSD_CHUNK, g, r, p)
    Bc = bm.reshape(b, nc, SSD_CHUNK, g, n)
    Cc = cm.reshape(b, nc, SSD_CHUNK, g, n)
    A = jnp.transpose(a_dt.reshape(b, nc, SSD_CHUNK, g, r), (0, 3, 4, 1, 2))
    A_cs = jnp.cumsum(A, axis=-1)
    Lm = segsum_exp(A)
    cb = jnp.einsum('bclgn,bcsgn->bgcls', Cc, Bc)
    y_diag = jnp.einsum('bgrcls,bcsgrp->bclgrp', cb[:, :, None] * Lm, X)
    decay_states = jnp.exp(A_cs[..., -1:] - A_cs)
    states = jnp.einsum('bcsgn,bgrcs,bcsgrp->bcgrpn', Bc, decay_states, X)
    states = jnp.concatenate([s0[:, None], states], axis=1)
    chunk_tot = jnp.pad(A_cs[..., -1], ((0, 0), (0, 0), (0, 0), (1, 0)))
    decay_chunk = segsum_exp(chunk_tot)
    new_states = jnp.einsum('bgrzc,bcgrpn->bzgrpn', decay_chunk, states)
    prev_states, final = new_states[:, :-1], new_states[:, -1]
    y_off = jnp.einsum('bclgn,bcgrpn,bgrcl->bclgrp', Cc, prev_states, jnp.exp(A_cs))
    return (y_diag + y_off).reshape(b, L, g, r, p), final

def hgrn2_chunked(q, k, v, log_f, s0):
    b, L, h, dk = q.shape
    dv = v.shape[-1]
    nc = L // HG_CHUNK

    def chunks(t):
        return jnp.moveaxis(t.reshape(b, nc, HG_CHUNK, h, t.shape[-1]), 1, 0)

    lower = jnp.tril(jnp.ones((HG_CHUNK, HG_CHUNK), dtype=bool))[None, :, :, None, None]

    def step(S, inp):
        qc, kc, vc, lc = inp
        bcum = jnp.cumsum(lc, axis=1)
        diff = bcum[:, :, None] - bcum[:, None, :]
        decay = jnp.where(lower, jnp.exp(jnp.where(lower, diff, 0.0)), 0.0)
        att = jnp.einsum('bthd,btshd->bths', qc, decay * kc[:, None])
        o = jnp.einsum('bths,bshv->bthv', att, vc) + jnp.einsum('bthd,bhdv->bthv', qc * jnp.exp(bcum), S)
        blast = bcum[:, -1]
        S_new = jnp.exp(blast)[..., None] * S + jnp.einsum('bshd,bshv->bhdv', kc * jnp.exp(blast[:, None] - bcum), vc)
        return S_new, o

    s_fin, o = lax.scan(step, s0, (chunks(q), chunks(k), chunks(v), chunks(log_f)))
    return jnp.moveaxis(o, 0, 1).reshape(b, L, h, dv), s_fin

def flip(t):
    return jnp.flip(t, axis=1)

def ssm_mixer(h, s_ssd, s_hg, w_in, conv_w, conv_b, dt_bias, a_log, d_skip, ssd_g, lb, hg_g, w_out):
    b, L, _ = h.shape
    f32 = jnp.float32
    proj = h @ w_in
    p0 = SSD_D_INNER
    p1 = p0 + SSD_XBC
    p2 = p1 + 2 * SSD_HEADS
    p3 = p2 + HG_D
    p4 = p3 + 2 * HG_D
    p5 = p4 + HG_D
    z, xbc, dt_raw, q, zf, v, og = jnp.split(proj, [p0, p1, p2, p3, p4, p5], axis=-1)
    xbc = jax.nn.silu(dwconv(xbc, conv_w, conv_b))
    xs, bm, cm = jnp.split(xbc, [SSD_D_INNER, SSD_D_INNER + SSD_GROUPS * SSD_STATE], axis=-1)
    xs32 = xs.astype(f32).reshape(b, L, SSD_GROUPS, SSD_HPG, SSD_HEAD_DIM)
    bm32 = bm.astype(f32).reshape(b, L, SSD_GROUPS, SSD_STATE)
    cm32 = cm.astype(f32).reshape(b, L, SSD_GROUPS, SSD_STATE)
    dt = jax.nn.softplus(dt_raw.astype(f32).reshape(b, L, 2, SSD_HEADS) + dt_bias.astype(f32))
    a = -jnp.exp(a_log.astype(f32))
    a_dt = (dt * a).reshape(b, L, 2, SSD_GROUPS, SSD_HPG)
    xdt = xs32[:, :, None] * dt.reshape(b, L, 2, SSD_GROUPS, SSD_HPG)[..., None]
    s0 = s_ssd.astype(f32).reshape(b, 2, SSD_GROUPS, SSD_HPG, SSD_HEAD_DIM, SSD_STATE)
    y_f, fin_f = ssd_chunked(xdt[:, :, 0], a_dt[:, :, 0], bm32, cm32, s0[:, 0])
    y_b, fin_b = ssd_chunked(flip(xdt[:, :, 1]), flip(a_dt[:, :, 1]), flip(bm32), flip(cm32), s0[:, 1])
    y = y_f + flip(y_b) + d_skip.astype(f32).reshape(SSD_GROUPS, SSD_HPG)[:, :, None] * xs32
    y_ssd = rms_norm(y.reshape(b, L, SSD_D_INNER) * jax.nn.silu(z.astype(f32)), ssd_g)
    new_ssd = jnp.stack([fin_f, fin_b], axis=1).reshape(b, 2, SSD_HEADS, SSD_HEAD_DIM, SSD_STATE)
    lb32 = lb.astype(f32)
    zf = zf.astype(f32).reshape(b, L, 2, HG_D)
    f_gate = lb32 + (1.0 - lb32) * jax.nn.sigmoid(zf)
    log_f = jnp.log(jnp.maximum(f_gate, F_FLOOR))
    k = (1.0 - lb32) * jax.nn.sigmoid(-zf)

    def heads(t):
        return t.reshape(b, L, HG_HEADS, HG_HEAD_DIM)

    qh = heads(jax.nn.silu(q.astype(f32)))
    vh = heads(v.astype(f32))
    sh = s_hg.astype(f32)
    o_f, hf_f = hgrn2_chunked(qh, heads(k[:, :, 0]), vh, heads(log_f[:, :, 0]), sh[:, 0])
    o_b, hf_b = hgrn2_chunked(flip(qh), heads(flip(k[:, :, 1])), flip(vh), heads(flip(log_f[:, :, 1])), sh[:, 1])
    o = rms_norm(o_f + flip(o_b), hg_g.reshape(HG_HEADS, HG_HEAD_DIM))
    y_hg = o.reshape(b, L, HG_D) * jax.nn.silu(og.astype(f32))
    new_hg = jnp.stack([hf_f, hf_b], axis=1)
    y_out = jnp.concatenate([y_ssd, y_hg], axis=-1).astype(h.dtype) @ w_out
    return y_out, new_ssd, new_hg

def axial_rope(L):
    rows = L // GRID_W
    row = jnp.repeat(jnp.arange(rows, dtype=jnp.float32), GRID_W)
    col = jnp.tile(jnp.arange(GRID_W, dtype=jnp.float32), rows)
    nf = ATTN_HEAD_DIM // 4
    inv = ROPE_THETA ** (-jnp.arange(nf, dtype=jnp.float32) / nf)
    ar = row[:, None] * inv
    ac = col[:, None] * inv
    return (jnp.cos(ar), jnp.sin(ar), jnp.cos(ac), jnp.sin(ac))

def rotate_half_block(x, cos, sin):
    x1, x2 = jnp.split(x, 2, axis=-1)
    cos = cos[:, None, :].astype(x.dtype)
    sin = sin[:, None, :].astype(x.dtype)
    return jnp.concatenate([x1 * cos - x2 * sin, x1 * sin + x2 * cos], axis=-1)

def apply_axial_rope(x, rope):
    cr, sr, cc, sc = rope
    xr, xc = jnp.split(x, 2, axis=-1)
    return jnp.concatenate([rotate_half_block(xr, cr, sr), rotate_half_block(xc, cc, sc)], axis=-1)

def attn_project(h, w_qkv, q_g, k_g):
    b, L, _ = h.shape
    q, k, v = jnp.split(h @ w_qkv, [ATTN_HEADS * ATTN_HEAD_DIM, (ATTN_HEADS + ATTN_KV_HEADS) * ATTN_HEAD_DIM], axis=-1)
    q = rms_norm(q.reshape(b, L, ATTN_HEADS, ATTN_HEAD_DIM), q_g)
    k = rms_norm(k.reshape(b, L, ATTN_KV_HEADS, ATTN_HEAD_DIM), k_g)
    return q, k, v.reshape(b, L, ATTN_KV_HEADS, ATTN_HEAD_DIM)

def block_attention(q, k, v):
    b, L, H, hd = q.shape
    nb = L // ATTN_BLOCK
    qb = q.reshape(b, nb, ATTN_BLOCK, ATTN_KV_HEADS, ATTN_GROUP, hd).transpose(1, 0, 3, 4, 2, 5)
    scale = hd ** -0.5

    def one(qblk):
        s = jnp.einsum('bkgqd,bksd->bkgqs', qblk, k).astype(jnp.float32) * scale
        p = jax.nn.softmax(s, axis=-1).astype(v.dtype)
        return jnp.einsum('bkgqs,bksd->bkgqd', p, v)

    o = lax.map(one, qb)
    return o.transpose(1, 0, 4, 2, 3, 5).reshape(b, L, H * hd)

def conv_ffn(h, w_up, conv_w, conv_b, w_down):
    u = dwconv(h @ w_up, conv_w, conv_b)
    gate, val = jnp.split(u, 2, axis=-1)
    return (jax.nn.silu(gate) * val) @ w_down

def setup_inputs(seed: int = 0) -> dict:
    key = jax.random.key(seed)
    ks = jax.random.split(key, 32)
    D = D_MODEL
    NS = N_SSM_LAYERS
    NA = N_ATTN_LAYERS

    def nrm(k, shape, s):
        return s * jax.random.normal(k, shape, jnp.float32)

    dt0 = jnp.exp(jax.random.uniform(ks[0], (NS, 2, SSD_HEADS), jnp.float32, math.log(1e-3), math.log(1e-1)))
    return {
        'x_prompt': nrm(ks[1], (BATCH, SEQ, D), 1.0),
        'x_sample': nrm(ks[2], (DEC_BATCH, DEC_SEQ, D), 1.0),
        'cache_k': nrm(ks[3], (DEC_BATCH, NA, ATTN_KV_HEADS, PAST_LEN, ATTN_HEAD_DIM), 1.0),
        'cache_v': nrm(ks[4], (DEC_BATCH, NA, ATTN_KV_HEADS, PAST_LEN, ATTN_HEAD_DIM), 1.0),
        'state_ssd': nrm(ks[5], (DEC_BATCH, NS, 2, SSD_HEADS, SSD_HEAD_DIM, SSD_STATE), 0.1),
        'state_hgrn': nrm(ks[6], (DEC_BATCH, NS, 2, HG_HEADS, HG_HEAD_DIM, HG_HEAD_DIM), 0.1),
        'c': nrm(ks[7], (DEC_BATCH, D), 1.0),
        'c_ctx': nrm(ks[8], (D,), 1.0),
        'ada_w': nrm(ks[9], (DEPTH, D, 6 * D), D ** -0.5),
        'ada_b': nrm(ks[10], (DEPTH, 6 * D), 0.02),
        'norm_g': 1.0 + nrm(ks[11], (DEPTH, 4, D), 0.02),
        'ssm_w_in': nrm(ks[12], (NS, D, SSM_IN), D ** -0.5),
        'ssd_conv_w': nrm(ks[13], (NS, SSD_CONV, SSD_XBC), SSD_CONV ** -0.5),
        'ssd_conv_b': nrm(ks[14], (NS, SSD_XBC), 0.02),
        'ssd_dt_bias': dt0 + jnp.log(-jnp.expm1(-dt0)),
        'ssd_a_log': jnp.log(jax.random.uniform(ks[15], (NS, 2, SSD_HEADS), jnp.float32, 1.0, 16.0)),
        'ssd_d': 1.0 + nrm(ks[16], (NS, SSD_HEADS), 0.1),
        'ssd_norm_g': 1.0 + nrm(ks[17], (NS, SSD_D_INNER), 0.02),
        'hg_lb_logits': nrm(ks[18], (2, NS, HG_D), 0.5),
        'hg_norm_g': 1.0 + nrm(ks[19], (NS, HG_D), 0.02),
        'ssm_w_out': nrm(ks[20], (NS, SSD_D_INNER + HG_D, D), (SSD_D_INNER + HG_D) ** -0.5),
        'attn_w_qkv': nrm(ks[21], (NA, D, ATTN_IN), D ** -0.5),
        'attn_q_norm': 1.0 + nrm(ks[22], (NA, ATTN_HEAD_DIM), 0.02),
        'attn_k_norm': 1.0 + nrm(ks[23], (NA, ATTN_HEAD_DIM), 0.02),
        'attn_w_out': nrm(ks[24], (NA, D, D), D ** -0.5),
        'ffn_w_up': nrm(ks[25], (DEPTH, D, 2 * FFN_DIM), D ** -0.5),
        'ffn_conv_w': nrm(ks[26], (DEPTH, FFN_CONV, 2 * FFN_DIM), FFN_CONV ** -0.5),
        'ffn_conv_b': nrm(ks[27], (DEPTH, 2 * FFN_DIM), 0.02),
        'ffn_w_down': nrm(ks[28], (DEPTH, FFN_DIM, D), FFN_DIM ** -0.5),
    }

def reference(x_prompt, x_sample, cache_k, cache_v, state_ssd, state_hgrn, c, c_ctx, ada_w, ada_b, norm_g,
              ssm_w_in, ssd_conv_w, ssd_conv_b, ssd_dt_bias, ssd_a_log, ssd_d, ssd_norm_g, hg_lb_logits,
              hg_norm_g, ssm_w_out, attn_w_qkv, attn_q_norm, attn_k_norm, attn_w_out, ffn_w_up, ffn_conv_w,
              ffn_conv_b, ffn_w_down):
    bp = x_prompt.shape[0]
    lb_p = jax.nn.softmax(hg_lb_logits.astype(jnp.float32), axis=1)
    lower_bounds = jnp.cumsum(lb_p, axis=1) - lb_p[:, :1]
    rope = axial_rope(x_sample.shape[1])
    xp, xs = x_prompt, x_sample
    new_k, new_v, new_ssd, new_hg = [], [], [], []
    for layer in range(DEPTH):
        g = norm_g[layer]
        sh_p, sc_p, gt_p, shf_p, scf_p, gtf_p = modulation(c_ctx[None, None, :], ada_w[layer], ada_b[layer])
        sh_s, sc_s, gt_s, shf_s, scf_s, gtf_s = modulation(c[:, None, :], ada_w[layer], ada_b[layer])
        j = layer // 2
        hp = adaln(xp, g[0], sh_p, sc_p)
        hs = adaln(xs, g[0], sh_s, sc_s)
        if layer % 2 == 0:
            prm = (ssm_w_in[j], ssd_conv_w[j], ssd_conv_b[j], ssd_dt_bias[j], ssd_a_log[j], ssd_d[j],
                   ssd_norm_g[j], lower_bounds[:, j], hg_norm_g[j], ssm_w_out[j])
            zs = jnp.zeros((bp, 2, SSD_HEADS, SSD_HEAD_DIM, SSD_STATE), jnp.float32)
            zh = jnp.zeros((bp, 2, HG_HEADS, HG_HEAD_DIM, HG_HEAD_DIM), jnp.float32)
            yp, s_ssd, s_hg = ssm_mixer(hp, zs, zh, *prm)
            new_ssd.append(s_ssd)
            new_hg.append(s_hg)
            ys, _, _ = ssm_mixer(hs, state_ssd[:, j], state_hgrn[:, j], *prm)
        else:
            qp, kp, vp = attn_project(hp, attn_w_qkv[j], attn_q_norm[j], attn_k_norm[j])
            kp = kp.transpose(0, 2, 1, 3)
            vp = vp.transpose(0, 2, 1, 3)
            yp = block_attention(qp, kp, vp) @ attn_w_out[j]
            new_k.append(kp)
            new_v.append(vp)
            qs, k_lat, v_lat = attn_project(hs, attn_w_qkv[j], attn_q_norm[j], attn_k_norm[j])
            qs = apply_axial_rope(qs, rope)
            k_lat = apply_axial_rope(k_lat, rope).transpose(0, 2, 1, 3)
            k_all = jnp.concatenate([k_lat, cache_k[:, j]], axis=2)
            v_all = jnp.concatenate([v_lat.transpose(0, 2, 1, 3), cache_v[:, j]], axis=2)
            ys = block_attention(qs, k_all, v_all) @ attn_w_out[j]
        xp = gated_residual(xp, yp, g[1], gt_p)
        xs = gated_residual(xs, ys, g[1], gt_s)
        fprm = (ffn_w_up[layer], ffn_conv_w[layer], ffn_conv_b[layer], ffn_w_down[layer])
        xp = gated_residual(xp, conv_ffn(adaln(xp, g[2], shf_p, scf_p), *fprm), g[3], gtf_p)
        xs = gated_residual(xs, conv_ffn(adaln(xs, g[2], shf_s, scf_s), *fprm), g[3], gtf_s)
    return (xp, xs, jnp.stack(new_k, axis=1), jnp.stack(new_v, axis=1), jnp.stack(new_ssd, axis=1), jnp.stack(new_hg, axis=1))


_drawn_inputs = setup_inputs


def setup_inputs(seed=0):
    import zlib

    import numpy as np

    out = dict(_drawn_inputs(seed))
    spreads = {}
    factors = {'state_hgrn': 64.0,
     'ssd_d': 3.685,
     'ssd_norm_g': 18.961,
     'hg_norm_g': 24.17,
     'attn_q_norm': 8.0,
     'attn_k_norm': 3.062,
     'ffn_conv_b': 4.183,
     'cache_k': 8.0,
     'cache_v': 8.0}
    for name, (base, spread) in spreads.items():
        noise = np.random.default_rng([zlib.crc32(name.encode()), seed]).standard_normal(out[name].shape)
        drawn = base * np.exp(spread * noise) if base else spread * noise
        out[name] = jnp.asarray(drawn.astype(out[name].dtype))
    for name, factor in factors.items():
        out[name] = (out[name] * factor).astype(out[name].dtype)
    return out
```

```python
from contextlib import ExitStack

import numpy as np
import concourse.bass as bass
from concourse import mybir

F32 = mybir.dt.float32
F32R = mybir.dt.float32r
U8 = mybir.dt.uint8
ALU = mybir.AluOpType
ACT = mybir.ActivationFunctionType
AX_X = mybir.AxisListType.X

P = 128
D_MODEL = 1024
KT = D_MODEL // P
SAMPLE, PROMPT = 512, 128
NT = SAMPLE + PROMPT
SEQS = ((0, SAMPLE, 1), (SAMPLE, NT, 0))
TT = NT // P
PROMPT_TT = TT - 1
EPS = 1e-6
F_FLOOR = 1e-30
HEADS_SSD, SSD_P, SSD_GROUPS = 16, 64, 2
HPG = HEADS_SSD // SSD_GROUPS
HG_HEADS, HG_SET = 8, 4
LEVELS = 7
ATTN_HEADS, KV_HEADS, HD = 16, 4, 64
FFN_T = 2816 // P
FFN_H = FFN_T // 2
RING = 4
ADA_RING = 2
N_ADA = 2 * 6 * KT
ADA_FIRST = 2 * KT
CP = NT + 1
UP = NT + 3

_SMALL = [("cond", KT * 2), ("ada_b", N_ADA), ("norm_g", 2 * 4 * KT), ("sconv_w", 3 * 12), ("sconv_b", 12),
          ("fconv_w", 2 * 3 * 44), ("fconv_b", 2 * 44), ("ssd_g", KT), ("hg_g", KT), ("ssd_d", KT),
          ("lb", 2 * KT), ("q_g", 1), ("k_g", 1), ("dt_b", 32), ("a_log", 32)]
SMALL = {}
_n = 0
for _name, _w in _SMALL:
    SMALL[_name] = (_n, _n + _w)
    _n += _w
N_SMALL = _n
IDENT, ONES, GT, LT, LE, GE, BD64, ROT = range(8)


def plan():
    tiles, slot = [], 0

    def full(kind, i):
        nonlocal slot
        tiles.append((kind, i, [(slot, k, k) for k in range(KT)]))
        slot += 1

    def ffn(layer):
        nonlocal slot
        for half in range(2):
            for i in range(FFN_H):
                full("gate", (layer, half * FFN_H + i))
                full("val", (layer, half * FFN_H + i))
            for m in range(KT):
                t = [(slot + (m * FFN_H + k) // KT, (m * FFN_H + k) % KT, k) for k in range(FFN_H)]
                tiles.append(("down", (layer, half, m), t))
            slot += FFN_H

    full("dt", 0)
    for g in range(SSD_GROUPS):
        for i in (8 + g, 10 + g, 4 * g, 4 * g + 1, 4 * g + 2, 4 * g + 3):
            full("conv", i)
        for i in range(4):
            full("z", 4 * g + i)
    for g in range(2):
        for i in range(4):
            full("q", 4 * g + i)
        for d in range(2):
            for i in range(4):
                full("zf", (d, 4 * g + i))
        for i in range(4):
            full("v", 4 * g + i)
    for i in range(KT):
        full("og", i)
    for half in (1, 0):
        for i in range(KT):
            full("out", (half, i))
    ffn(0)
    for i in range(8):
        full("aq", i)
    for i in range(4):
        full("ak", i)
    for i in range(2):
        full("av", i)
    for i in range(KT):
        full("aout", i)
    ffn(1)
    return tiles, slot


TILES, N_SLOTS = plan()
LAST_TILE = {}
for _t, (_k, _i, _kts) in enumerate(TILES):
    for _s, _, _ in _kts:
        LAST_TILE[_s] = _t
MID_SLOTS = [_s for _s in range(N_SLOTS) if TILES[LAST_TILE[_s]][2][-1][0] != _s]
MID_COUNT = {_s: _n + 1 for _n, _s in enumerate(MID_SLOTS)}
FIRST_OF = {}
for _t, (_k, _i, _kts) in enumerate(TILES):
    FIRST_OF.setdefault(_k, _t)
    FIRST_OF.setdefault((_k, _i[0] if isinstance(_i, tuple) else _i), _t)
    FIRST_OF.setdefault((_k, _i), _t)

def ada_after(t):
    a = ADA_FIRST + t
    return a if a < N_ADA else None


NORMS = [8] + [1] * 8 + [8] + [8, 8, 8, 8] + [1] * 12 + [8, 8, 8]
N_ADALN0, N_HG, N_SSD, N_RES0, N_FFN0, N_RES1, N_ATT, N_QK, N_RES2, N_FFN1, N_RES3 = 0, 1, 9, 10, 11, 12, 13, 14, 26, 27, 28
NORM_BASE = [sum(NORMS[:i]) for i in range(len(NORMS) + 1)]

HG_PAIRS = [(PROMPT_TT, PROMPT_TT), (0, 3), (1, 2), (2, 1), (3, 0)]
SSD_STATES = [(0, PROMPT_TT), (1, PROMPT_TT), (0, 0), (1, 3), (0, 1), (1, 2), (0, 2), (1, 1)]
SSD_UNITS = [(t, q) for t in (PROMPT_TT, 0, 1, 2, 3) for q in range(2)]
ATT_UNITS = [(h, b) for h in range(ATTN_HEADS) for b in range(TT)]


def hybrid_step(nc, x, cond_small, consts, masks8, rope, s_ssd, s_hg, cache_k, cache_v, wstream, wada,
                y_out, k_out, v_out, ssd_out, hg_out):
    yssd_dram = nc.dram_tensor("yssd_scratch", [P, KT * NT], F32).ap()
    with ExitStack() as ctx:
        def sb(name, shape, dt=F32, stack=ctx):
            return stack.enter_context(nc.sbuf_tensor(name, shape, dt))

        def sem(name):
            return ctx.enter_context(nc.semaphore(name))

        ring = sb("ring", [P, RING, KT, P])
        adaring = sb("adaring", [P, ADA_RING, KT, P])
        whi = sb("whi", [P, 2, KT, P], F32R)
        wlo = sb("wlo", [P, 2, KT, P], F32R)
        hh = sb("hh", [P, KT, NT], F32R)
        hl = sb("hl", [P, KT, NT], F32R)
        ybuf = sb("ybuf", [P, KT, NT])
        sq = sb("sq", [P, 2, NT + 2])
        rt = sb("rt", [P, NT])
        rb = sb("rb", [P, NT])
        wk = sb("wk", [P, 4, NT + 4])
        cm = sb("cm", [P, 8, P])
        m8 = sb("m8", [P, 2 * LEVELS * 64 + P], U8)
        small = sb("small", [P, N_SMALL])
        mod = sb("mod", [P, N_ADA, 2])
        condT = sb("condT", [P, KT, 2])
        scal = sb("scal", [P, 6, KT, 2])
        lbt = sb("lbt", [P, 4, 2 * KT])

        def par(name, a=None, b=None):
            lo, hi = SMALL[name]
            return small[:, lo:hi] if a is None else small[:, lo + a:lo + (a + 1 if b is None else b)]

        with ExitStack() as ph:
            xsT = sb("xsT", [P, 4, NT], F32, ph)
            bcT = sb("bcT", [P, 2, NT], F32, ph)
            zs = sb("zs", [P, 4, NT], F32, ph)
            xtok = sb("xtok", [P, TT, 512], F32, ph)
            btok = sb("btok", [P, TT, P], F32, ph)
            st = sb("st", [P, 2, 4, 512], F32, ph)
            ra = sb("ra", [P, 2, 4, P], F32, ph)
            eg = sb("eg", [P, 2, 4, P], F32, ph)
            ec = sb("ec", [P, 2, 4, P], F32, ph)
            xd = sb("xd", [P, 2, 512], F32, ph)
            cbm = sb("cbm", [P, 2, P], F32, ph)
            dtt = sb("dtt", [P, TT, 32], F32, ph)
            adt = sb("adt", [P, TT, 32], F32, ph)
            dtw = sb("dtw", [P, 3, TT, 32], F32, ph)
            eal = sb("eal", [P, 32], F32, ph)
            dect = sb("dect", [P, 4, TT, HPG], F32, ph)
            wdec = sb("wdec", [P, 2, TT, HPG], F32, ph)
        with ExitStack() as ph:
            qs = sb("qs", [P, HG_SET, NT], F32, ph)
            fg = sb("fg", [P, 2, HG_SET, NT], F32, ph)
            kg = sb("kg", [P, 2, HG_SET, NT], F32, ph)
            vtok = sb("vtok", [P, TT, HG_SET * P], F32, ph)
            tp = sb("tp", [P, 2, HG_SET, P], F32, ph)
            att = sb("att", [P, 2, HG_SET, P], F32, ph)
            hst = sb("hst", [P, 2, HG_SET, P], F32, ph)
            hfin = sb("hfin", [P, 2, HG_SET, P], F32, ph)
        qp = wk[:, 0:2, 0:HG_SET * P].rearrange("p d (h t) -> p d h t", h=HG_SET)
        ktok = wk[:, 2:4, 0:HG_SET * P].rearrange("p d (h t) -> p d h t", h=HG_SET)
        mask_in = ybuf[:, 0:2].rearrange("p f t -> p (f t)")[:, 0:2 * LEVELS * 64 + P]
        sfin, xw = sq[:, 0, 0:512], sq[:, 1, 0:512]
        xT = sb("xT", [P, KT, NT])
        with ExitStack() as ph:
            gh = sb("gh", [P, FFN_H, NT + 2], F32R, ph)
            gl = sb("gl", [P, FFN_H, NT + 2], F32R, ph)
        with ExitStack() as ph:
            aq = sb("aq", [P, 8, NT], F32, ph)
            ak = sb("ak", [P, KV_HEADS, NT + P], F32, ph)
            av = sb("av", [P, TT + 1, KV_HEADS * HD], F32, ph)
            pr = sb("pr", [P, 2, NT], F32, ph)
            pt = sb("pt", [P, 2, TT, P], F32, ph)
            cs = sb("cs", [P, 2, SAMPLE], F32, ph)
            ck = sb("ck", [P, KV_HEADS, 2, HD], F32, ph)
            kout = sb("kout", [P, KV_HEADS, HD], F32, ph)
            mxs = sb("mxs", [P, 2, 4], F32, ph)

        pg = ctx.enter_context(nc.psum_tensor("pg", [P, 2, 1024], F32))
        ps = ctx.enter_context(nc.psum_tensor("ps", [P, 4, 512], F32))
        pn = ps[:, 2:4, :].rearrange("p a b -> p (a b)")[:, 0:NT]

        def pada(a):
            if a < ADA_FIRST:
                return pg[:, a // 2 % 2, a % 2 * 512:a % 2 * 512 + 2]
            return pg[:, a % 2, 768:770]


        small_in = sem("small_in")
        x_in = sem("x_in")
        x_again = sem("x_again")
        w_loaded = [sem(f"w_loaded{i}") for i in range(RING)]
        ada_loaded = [sem(f"ada_loaded{i}") for i in range(ADA_RING)]
        whi_ready = sem("whi_ready")
        wlo_ready = sem("wlo_ready")
        part_used = sem("part_used")
        tile_ready = sem("tile_ready")
        tile_free = [sem(f"tile_free{i}") for i in range(2)]
        cond_ready = sem("cond_ready")
        ada_ready = sem("ada_ready")
        mod_ready = sem("mod_ready")
        sq_ready = sem("sq_ready")
        nsum_ready = sem("nsum_ready")
        rt_ready = sem("rt_ready")
        r_ready = sem("r_ready")
        t_ready = sem("t_ready")
        aff_ready = sem("aff_ready")
        h_ready = sem("h_ready")
        x_ready = sem("x_ready")
        conv_ready = sem("conv_ready")
        conv_done = sem("conv_done")
        g_ready = sem("g_ready")
        dt_abs = sem("dt_abs")
        dt_log = sem("dt_log")
        dt_ready = sem("dt_ready")
        tr_ready = sem("tr_ready")
        tr_done = sem("tr_done")
        s0_in = sem("s0_in")
        dsum_ready = sem("dsum_ready")
        dexp_ready = sem("dexp_ready")
        xw_ready = sem("xw_ready")
        ls_ready = sem("ls_ready")
        st_ready = sem("st_ready")
        sfin_out = sem("sfin_out")
        cb_ready = sem("cb_ready")
        ra_ready = sem("ra_ready")
        dd_ready = sem("dd_ready")
        ex_ready = sem("ex_ready")
        exc_ready = sem("exc_ready")
        g_done = sem("g_done")
        cs_ready = sem("cs_ready")
        yu_ready = sem("yu_ready")
        yu_done = sem("yu_done")
        yd_ready = sem("yd_ready")
        yz_ready = sem("yz_ready")
        yssd_out = sem("yssd_out")
        yssd_in = sem("yssd_in")
        lb_d = sem("lb_d")
        lb_e = sem("lb_e")
        fk_ready = sem("fk_ready")
        att_zero = sem("att_zero")
        qp_ready = sem("qp_ready")
        dg_ready = sem("dg_ready")
        lv_ready = sem("lv_ready")
        kk_ready = sem("kk_ready")
        kt_ready = sem("kt_ready")
        kt_done = sem("kt_done")
        o_ready = sem("o_ready")
        o_done = [sem(f"o_done{i}") for i in range(2)]
        hs_ready = sem("hs_ready")
        hs_done = sem("hs_done")
        hst_in = sem("hst_in")
        hfin_out = sem("hfin_out")
        og_done = sem("og_done")
        kv_in = sem("kv_in")
        qk_norm = sem("qk_norm")
        rot_ready = sem("rot_ready")
        rope_done = sem("rope_done")
        ko_ready = sem("ko_ready")
        sc_ready = sem("sc_ready")
        mx_ready = sem("mx_ready")
        pe_exp = sem("pe_exp")
        pr_ready = sem("pr_ready")
        pt_ready = sem("pt_ready")
        pt_done = sem("pt_done")
        ao_ready = sem("ao_ready")
        ao_done = sem("ao_done")
        kv_out = sem("kv_out")
        y_written = sem("y_written")
        vch = sem("vector_chain")
        ach = sem("scalar_chain")

        block = ctx.enter_context(nc.Block())

        def modulated(eng, i):
            if i <= ADA_FIRST:
                eng.wait_ge(mod_ready, i)
            else:
                for b in range(2):
                    eng.wait_ge(tile_free[b], freed(b, i - ADA_FIRST))

        def conv_cols(a):
            return a[:, 0:SAMPLE], a[:, SAMPLE + 1:CP]

        def halves(ap, w, t):
            return ap.rearrange("p h (b t w) -> p h b t w", t=2, w=w)[:, :, :, t, :]

        def tlevel(d, i):
            off = P - (P >> (i - 1))
            return tp[:, d, :, off:off + (P >> i)]

        def mod_at(layer, part, ft, c):
            i = (layer * 6 + part) * KT + ft
            return mod[:, i, c:c + 1]

        @block.sync
        def _(sp):
            sp.dma_start(small[:], cond_small).then_inc(small_in, 16)
            sp.dma_start(cm[:], consts).then_inc(small_in, 16)
            sp.dma_start(mask_in, masks8).then_inc(small_in, 16)
            sp.dma_start(xT[:], x).then_inc(x_in, 16)

            def load_ada(a):
                if a >= ADA_FIRST + ADA_RING:
                    sp.wait_ge(tile_ready, a - ADA_FIRST - ADA_RING + 1)
                elif a >= ADA_RING:
                    sp.wait_ge(ada_ready, a - ADA_RING + 1)
                sp.dma_start(adaring[:, a % ADA_RING], wada[a]).then_inc(ada_loaded[a % ADA_RING], 16)

            def load_w(s):
                if s >= RING:
                    sp.wait_ge(wlo_ready, s - RING + 1)
                sp.dma_start(ring[:, s % RING], wstream[s]).then_inc(w_loaded[s % RING], 16)

            for a in range(ADA_FIRST):
                load_ada(a)
            for s in range(RING - 1):
                load_w(s)
            at = 0
            for s in range(RING - 1, N_SLOTS):
                load_w(s)
                a = ada_after(at)
                if a is not None and LAST_TILE.get(s - 2, -1) >= at:
                    load_ada(a)
                    at += 1

        @block.tensor
        def _(pe):
            def ada(a):
                pe.wait_ge(ada_loaded[a % ADA_RING], 16 * (a // ADA_RING + 1))
                if 4 <= a < ADA_FIRST:
                    pe.wait_ge(mod_ready, a - 3)
                for k in range(KT):
                    last = nc.tensor.matmul(pada(a), adaring[:, a % ADA_RING, k, :], condT[:, k, :],
                                            start=k == 0, stop=k == KT - 1)
                last.then_inc(ada_ready if a < ADA_FIRST else tile_ready, 1)

            def gemm(t, h_base=None, g_base=None):
                kind, _, kts = TILES[t]
                out = pg[:, t % 2, 0:NT]
                if t >= 2:
                    pe.wait_ge(tile_free[t % 2], t // 2)
                hi, lo = (gh, gl) if kind == "down" else (hh, hl)
                if kind in ("dt", "v", "av"):
                    pe.wait_ge(wlo_ready, kts[0][0] + 1)
                    if h_base is not None:
                        pe.wait_ge(h_ready, h_base + KT)
                    s = kts[0][0] % 2
                    for tt in range(TT):
                        tok = slice(tt * P, (tt + 1) * P)
                        for k in range(KT):
                            for n, (a, w) in enumerate(((hi, whi), (lo, whi), (hi, wlo))):
                                last = nc.tensor.matmul(out[:, tok], a[:, k, tok], w[:, s, k, :],
                                                        start=k == 0 and n == 0, stop=k == KT - 1 and n == 2)
                else:
                    seen = -1
                    for n, (s, pos, k) in enumerate(kts):
                        if s > seen:
                            pe.wait_ge(wlo_ready, s + 1)
                            seen = s
                        if h_base is not None:
                            pe.wait_ge(h_ready, h_base + k + 1)
                        if g_base is not None:
                            pe.wait_ge(g_ready, g_base + k + 1)
                        for m, (a, w) in enumerate(((hi, whi), (lo, whi), (hi, wlo))):
                            for lo_t, hi_t, _ in SEQS:
                                gap = 1 if kind == "down" and lo_t else 0
                                last = nc.tensor.matmul(out[:, lo_t:hi_t], w[:, s % 2, pos, :],
                                                        a[:, k, lo_t + gap:hi_t + gap],
                                                        start=n == 0 and m == 0, stop=n == len(kts) - 1 and m == 2)
                        if s in MID_COUNT and LAST_TILE[s] == t and kts[n + 1][0] != s:
                            last.then_inc(part_used, 1)
                a = ada_after(t)
                if a is not None:
                    ada(a)
                else:
                    last.then_inc(tile_ready, 1)

            def norm(n, which=ONES):
                if n >= 1:
                    pe.wait_ge(rt_ready, n)
                for i in range(NORMS[n]):
                    c = NORM_BASE[n] + i
                    pe.wait_ge(sq_ready, c + 1)
                    for lo_t, hi_t, _ in SEQS:
                        last = nc.tensor.matmul(pn[:, lo_t:hi_t], cm[:, which, :], sq[:, c % 2, lo_t:hi_t],
                                                start=i == 0, stop=i == NORMS[n] - 1)
                    last.then_inc(nsum_ready, 1)

            def transposes(j, jobs):
                if j >= 2:
                    pe.wait_ge(tr_done, j - 1)
                for i, src in enumerate(jobs):
                    last = nc.tensor.transpose(ps[:, j % 2, i * P:(i + 1) * P], src, cm[:, IDENT, :])
                last.then_inc(tr_ready, 1)

            def ssd(g):
                pe.wait_ge(conv_done, 6 * (g + 1))
                j = 7 * g
                tok = lambda t: slice(t * P, (t + 1) * P)
                transposes(j, [bcT[:, 0, tok(t)] for t in range(4)])
                transposes(j + 1, [bcT[:, 0, tok(4)]])
                for t in range(TT):
                    transposes(j + 2 + t, [xsT[:, i, tok(t)] for i in range(4)])
                pe.wait_ge(dt_ready, 1)
                for d in range(2):
                    a = adt[:, :, d * 16 + HPG * g:d * 16 + HPG * (g + 1)]
                    for n, m in enumerate(((GT, LT)[d], ONES)):
                        o = (2 * d + n) * TT * HPG
                        last = nc.tensor.matmul(ps[:, 2, o:o + TT * HPG].rearrange("p (t h) -> p t h", t=TT),
                                                cm[:, m, :], a, start=True, stop=True)
                last.then_inc(dsum_ready, 1)
                for n, (d, t) in enumerate(SSD_STATES):
                    n += g * len(SSD_STATES)
                    pe.wait_ge(xw_ready, n + 1)
                    if n:
                        pe.wait_ge(st_ready, n)
                    if d == 0 and t == PROMPT_TT:
                        pe.wait_ge(tr_done, 7 * (g + 1))
                    nc.tensor.matmul(ps[:, 3, :], btok[:, t, :], xw, start=True, stop=True).then_inc(ls_ready, 1)
                pe.wait_ge(st_ready, (g + 1) * len(SSD_STATES))
                pe.wait_ge(dexp_ready, g + 1)
                for n, (t, q) in enumerate(SSD_UNITS):
                    u = g * len(SSD_UNITS) + n
                    if q == 0:
                        if u:
                            pe.wait_ge(g_done, 2 * u)
                        nc.tensor.matmul(ps[:, 2, 0:P], bcT[:, 0, tok(t)], bcT[:, 1, tok(t)],
                                         start=True, stop=True).then_inc(cb_ready, 1)
                    for d in range(2):
                        v = 2 * u + d
                        pe.wait_ge(ra_ready, v + 1)
                        if v:
                            pe.wait_ge(exc_ready, v)
                        nc.tensor.matmul(ps[:, 0, :], cm[:, (GT, LT)[d], :], ra[:, d].rearrange("p h t -> p (h t)"),
                                         start=True, stop=True)
                        nc.tensor.matmul(ps[:, 1, :], cm[:, ONES, :], ra[:, d].rearrange("p h t -> p (h t)"),
                                         start=True, stop=True).then_inc(dd_ready, 1)
                    pe.wait_ge(g_done, 2 * u + 2)
                    pe.wait_ge(cs_ready, 2 * u + 2)
                    if u:
                        pe.wait_ge(yu_done, u)
                    for h in range(4):
                        o = ps[64 * (h % 2):64 * (h % 2) + 64, 3, (h // 2) * P:(h // 2 + 1) * P]
                        hp = slice((4 * q + h) * SSD_P, (4 * q + h + 1) * SSD_P)
                        for d in range(2):
                            off = t != PROMPT_TT
                            last = nc.tensor.matmul(o, xd[:, d, hp], eg[:, d, h, :], start=d == 0,
                                                    stop=d == 1 and not off, skip_group_check=True)
                            if off:
                                last = nc.tensor.matmul(o, st[:, d, t, hp], ec[:, d, h, :], start=False,
                                                        stop=d == 1, skip_group_check=True)
                    last.then_inc(yu_ready, 1)

            def hgrn(g):
                pe.wait_ge(fk_ready, 8 * (g + 1))
                for b in range(2):
                    pe.wait_ge(tile_free[b], freed(b, FIRST_OF[("v", 4 * g)] + 4))
                for p, pair in enumerate(HG_PAIRS):
                    np_ = g * len(HG_PAIRS) + p
                    tok = [slice(t * P, (t + 1) * P) for t in pair]
                    for d in range(2):
                        if np_:
                            pe.wait_ge(qp_ready, qp_need(np_ - 1, 0, 0))
                        for h in range(HG_SET):
                            last = nc.tensor.matmul(pg[:, 0, d * 512 + h * P:d * 512 + (h + 1) * P], kg[:, d, h, tok[d]],
                                                    qs[:, h, tok[d]], start=True, stop=True)
                        last.then_inc(dg_ready, 1)
                    for i in range(LEVELS):
                        for d in range(2):
                            n = (np_ * LEVELS + i) * 2 + d
                            pe.wait_ge(qp_ready, qp_need(np_, i, d))
                            if i:
                                pe.wait_ge(kk_ready, n - 1)
                            w = 1 << i
                            for h in range(HG_SET):
                                src = qp[:, d, h, :].rearrange("p (b t w) -> p b t w", t=2, w=w)[:, :, 1 - d, :]
                                last = nc.tensor.matmul(
                                    ps[:, d, h * 64:(h + 1) * 64],
                                    kg[:, d, h, tok[d]], src, start=True, stop=True)
                            last.then_inc(lv_ready, 1)
                    for d in range(2):
                        v = 2 * (np_ - g) + d
                        pe.wait_ge(qp_ready, qp_need(np_, LEVELS, d))
                        if p == len(HG_PAIRS) - 1:
                            continue
                        pe.wait_ge(kk_ready, 2 * LEVELS * np_ + 2 * (LEVELS - 1) + d + 1)
                        if v >= 2:
                            pe.wait_ge(kt_done, v - 1)
                        for h in range(HG_SET):
                            last = nc.tensor.transpose(pg[:, 1, d * 512 + h * P:d * 512 + (h + 1) * P], kg[:, d, h, tok[d]],
                                                       cm[:, IDENT, :])
                        last.then_inc(kt_ready, 1)
                    for d in range(2):
                        v = 2 * np_ + d
                        if v:
                            pe.wait_ge(o_done[(d + 1) % 2], np_ + (1 if d else 0))
                        if p == 1:
                            pe.wait_ge(hst_in, 16 * (g + 1))
                        for h in range(HG_SET):
                            o = ps[:, 2, h * P:(h + 1) * P]
                            last = nc.tensor.matmul(o, vtok[:, pair[d], h * P:(h + 1) * P], att[:, d, h, :],
                                                    start=True, stop=p == 0)
                            if p:
                                last = nc.tensor.matmul(o, hst[:, d, h, :], qp[:, d, h, :], start=False, stop=True)
                        last.then_inc(o_ready, 1)
                    if p < len(HG_PAIRS) - 1:
                        for d in range(2):
                            v = 2 * (np_ - g) + d
                            pe.wait_ge(kt_done, v + 1)
                            if v:
                                pe.wait_ge(hs_done, v)
                            for h in range(HG_SET):
                                last = nc.tensor.matmul(ps[:, 3, h * P:(h + 1) * P], ktok[:, d, h, :],
                                                        vtok[:, pair[d], h * P:(h + 1) * P], start=True, stop=True)
                            last.then_inc(hs_ready, 1)

            def ffn(layer):
                for half in range(2):
                    t0 = FIRST_OF[("gate", (layer, half * FFN_H))]
                    for i in range(2 * FFN_H):
                        gemm(t0 + i, h_base=H_BASE["ffn0" if layer == 0 else "ffn1"] if not half and not i else None)
                    for m in range(KT):
                        gemm(t0 + 2 * FFN_H + m, g_base=(2 * layer + half) * FFN_H if m == 0 else None)

            pe.wait_ge(small_in, 48)
            pe.wait_ge(cond_ready, 1)
            for a in range(ADA_FIRST):
                ada(a)
            norm(N_ADALN0)
            t = 0
            for g in range(SSD_GROUPS):
                for _ in range(11 if g == 0 else 10):
                    gemm(t, h_base=0 if t == 0 else None)
                    t += 1
                ssd(g)
            pe.wait_ge(att_zero, 1)
            pe.wait_ge(yu_done, 2 * len(SSD_UNITS))
            for g in range(2):
                for _ in range(16):
                    gemm(t)
                    t += 1
                hgrn(g)
            for h in range(KT):
                gemm(t)
                t += 1
                if h == 0:
                    for d in range(2):
                        pe.wait_ge(o_done[d], 10)
                    pe.wait_ge(hs_done, 16)
                norm(N_HG + h)
            for m in range(KT):
                gemm(t, h_base=H_BASE["hg"] if m == 0 else None)
                t += 1
            norm(N_SSD)
            for m in range(KT):
                gemm(t, h_base=H_BASE["ssd"] if m == 0 else None)
                t += 1
            norm(N_RES0)
            norm(N_FFN0)
            ffn(0)
            norm(N_RES1)
            norm(N_ATT)
            t = FIRST_OF["aq"]
            for i in range(14 + 2):
                if i < 14:
                    gemm(t + i, h_base=H_BASE["att"] if i == 0 else None)
                if 1 <= i <= 12:
                    norm(N_QK + i - 1, BD64)
                if 2 <= i <= 13:
                    j = i - 2
                    pe.wait_ge(qk_norm, j + 1)
                    if j:
                        pe.wait_ge(rope_done, j)
                    src = aq[:, j, 0:SAMPLE] if j < 8 else ak[:, j - 8, 0:SAMPLE]
                    nc.tensor.matmul(ps[:, 1, :], cm[:, ROT, :], src, start=True, stop=True).then_inc(rot_ready, 1)
            pe.wait_ge(rope_done, 12)
            pe.wait_ge(kv_in, 16 * 5)
            transposes(14, [ck[:, kv].rearrange("p a b -> p (a b)") for kv in range(KV_HEADS)])
            transposes(15, [ak[:, kv, SAMPLE:NT] for kv in range(KV_HEADS)])
            pe.wait_ge(tr_done, 16)
            for b in range(2):
                pe.wait_ge(tile_free[b], freed(b, FIRST_OF["aout"]))

            def keys(b):
                if b == PROMPT_TT:
                    return [(0, P, SAMPLE)], [PROMPT_TT]
                return [(0, SAMPLE, 0), (SAMPLE, NT, NT)], [0, 1, 2, 3, 5]

            def att_scores(u):
                h, b = ATT_UNITS[u]
                kv, r = h // (ATTN_HEADS // KV_HEADS), HD * (h % 2)
                if u >= 2:
                    pe.wait_ge(pe_exp, u - 1)
                for c0, c1, k0 in keys(b)[0]:
                    last = nc.tensor.matmul(pg[:, u % 2, c0:c1], aq[r:r + HD, h // 2, b * P:(b + 1) * P],
                                            ak[r:r + HD, kv, k0:k0 + c1 - c0], start=True, stop=True)
                last.then_inc(sc_ready, 1)

            def att_out(u):
                h, b = ATT_UNITS[u]
                kv, r = h // (ATTN_HEADS // KV_HEADS), HD * (h % 2)
                vt = keys(b)[1]
                pe.wait_ge(pr_ready, u + 1)
                if u:
                    pe.wait_ge(pt_done, u)
                bank = ps[:, 0:2, :].rearrange("p a b -> p (a b)")
                for j in range(len(vt)):
                    last = nc.tensor.transpose(bank[:, j * P:(j + 1) * P], pr[:, u % 2, j * P:(j + 1) * P],
                                               cm[:, IDENT, :])
                last.then_inc(pt_ready, 1)

            def att_pv(u):
                h, b = ATT_UNITS[u]
                kv, r = h // (ATTN_HEADS // KV_HEADS), HD * (h % 2)
                vt = keys(b)[1]
                pe.wait_ge(pt_done, u + 1)
                if u >= 2:
                    pe.wait_ge(ao_done, u - 1)
                for j, v in enumerate(vt):
                    last = nc.tensor.matmul(ps[r:r + HD, 2 + u % 2, 0:P], av[:, v, kv * HD:(kv + 1) * HD],
                                            pt[:, u % 2, j, :], start=j == 0, stop=j == len(vt) - 1)
                last.then_inc(ao_ready, 1)

            nu = len(ATT_UNITS)
            for u in range(nu + 2):
                if u < nu:
                    att_scores(u)
                if 1 <= u <= nu:
                    att_out(u - 1)
                if u >= 2:
                    att_pv(u - 2)
            t = FIRST_OF["aout"]
            for m in range(KT):
                if m < 2:
                    pe.wait_ge(pe_exp, nu)
                gemm(t + m, h_base=H_BASE["ao"] if m == 0 else None)
            norm(N_RES2)
            norm(N_FFN1)
            ffn(1)
            norm(N_RES3)

        @block.scalar
        def _(act):
            chain = [0]
            prepped = [0]

            def link(ins):
                chain[0] += 1
                ins.then_inc(ach, 1)
                act.wait_ge(ach, chain[0])

            def prep(t):
                upto = min(TILES[t][2][-1][0] + 2, N_SLOTS)
                for s in range(prepped[0], upto):
                    act.wait_ge(w_loaded[s % RING], 16 * (s // RING + 1))
                    if s >= 2:
                        if s - 2 in MID_COUNT:
                            act.wait_ge(part_used, MID_COUNT[s - 2])
                        else:
                            act.wait_ge(tile_ready, LAST_TILE[s - 2] + 1)
                    nc.scalar.copy(whi[:, s % 2], ring[:, s % RING]).then_inc(whi_ready, 1)
                prepped[0] = max(prepped[0], upto)

            def squares(n, src, waits):
                for i in range(NORMS[n]):
                    c = NORM_BASE[n] + i
                    waits(i)
                    if c >= 2:
                        act.wait_ge(nsum_ready, c - 1)
                    nc.scalar.activation(sq[:, c % 2, 0:NT], src(i), ACT.Square).then_inc(sq_ready, 1)

            def root(n, width):
                act.wait_ge(nsum_ready, NORM_BASE[n + 1])
                if n:
                    act.wait_ge(r_ready, n)
                nc.scalar.activation(rt[:], pn, ACT.Sqrt, scale=1.0 / width, bias=EPS).then_inc(rt_ready, 1)

            def affine(k, layer, which, base):
                modulated(act, (layer * 6 + 3 * which + 2) * KT)
                for ft in range(KT):
                    n = k * KT + ft
                    act.wait_ge(t_ready, n + 1)
                    if ft >= 2:
                        act.wait_ge(h_ready, base + ft - 1)
                    for lo, hi, c in SEQS:
                        last = nc.scalar.activation(wk[:, 2 + ft % 2, lo:hi], wk[:, ft % 2, lo:hi], ACT.Identity,
                                                    scale=scal[:, 0, ft, c:c + 1],
                                                    bias=mod_at(layer, 3 * which, ft, c))
                    last.then_inc(aff_ready, 1)

            def arrived(t):
                act.wait_ge(tile_ready, t + 1)
                a = ada_after(t)
                if a is not None:
                    nc.scalar.activation(mod[:, a, :], pada(a), ACT.Identity, bias=par("ada_b", a))

            def conv_in(t, n):
                if n >= 2:
                    act.wait_ge(conv_ready, n - 1)
                arrived(t)
                nc.scalar.copy(wk[:, n % 2, 1:SAMPLE + 1], pg[:, t % 2, 0:SAMPLE])
                nc.scalar.copy(wk[:, n % 2, SAMPLE + 2:UP - 1], pg[:, t % 2, SAMPLE:NT]).then_inc(tile_free[t % 2], 1)

            def evac(t, dst, func=ACT.Copy, scale=1.0):
                arrived(t)
                nc.scalar.activation(dst, pg[:, t % 2, 0:NT], func, scale=scale).then_inc(tile_free[t % 2], 1)

            def tr_evac(j, dst, n):
                act.wait_ge(tr_ready, j + 1)
                nc.scalar.copy(dst, ps[:, j % 2, 0:n]).then_inc(tr_done, 1)

            def ssd(g):
                j = 7 * g
                if g:
                    act.wait_ge(yz_ready, 1)
                for i in range(4):
                    if i == 0:
                        act.wait_ge(conv_done, 6 * (g + 1))
                    last = nc.scalar.activation(ybuf[:, 4 * g + i], xsT[:, i], ACT.Copy,
                                                scale=par("ssd_d", 4 * g + i))
                last.then_inc(yd_ready, 1)
                tr_evac(j, btok[:, 0:4].rearrange("p t n -> p (t n)"), 4 * P)
                tr_evac(j + 1, btok[:, 4], P)
                for t in range(TT):
                    tr_evac(j + 2 + t, xtok[:, t], 4 * P)
                act.wait_ge(dsum_ready, g + 1)
                nc.scalar.activation(dect[:].rearrange("p a t h -> p (a t h)"), ps[:, 2, 0:4 * TT * HPG],
                                     ACT.Exp).then_inc(dexp_ready, 1)
                for n in range(len(SSD_UNITS)):
                    u = g * len(SSD_UNITS) + n
                    for d in range(2):
                        v = 2 * u + d
                        act.wait_ge(dd_ready, v + 1)
                        if u:
                            act.wait_ge(yu_ready, u)
                        nc.scalar.activation(eg[:, d].rearrange("p h t -> p (h t)"), ps[:, 0, :],
                                             ACT.Exp).then_inc(ex_ready, 1)
                        nc.scalar.activation(ec[:, d].rearrange("p h t -> p (h t)"), ps[:, 1, :],
                                             ACT.Exp).then_inc(exc_ready, 1)

            def hgrn(g):
                for p, pair in enumerate(HG_PAIRS):
                    np_ = g * len(HG_PAIRS) + p
                    for d in range(2 if p < len(HG_PAIRS) - 1 else 0):
                        v = 2 * (np_ - g) + d
                        act.wait_ge(kt_ready, v + 1)
                        if v >= 2:
                            act.wait_ge(hs_ready, 2 * (np_ - g))
                        nc.scalar.copy(ktok[:, d].rearrange("p h t -> p (h t)"),
                                       pg[:, 1, d * 512:(d + 1) * 512]).then_inc(kt_done, 1)
                    for d in range(2):
                        v = 2 * np_ + d
                        if not (p in (1, 2) or (p == 0 and d == 0)):
                            continue
                        if v == 0:
                            act.wait_ge(yssd_out, 32)
                        act.wait_ge(o_ready, v + 1)
                        nc.scalar.copy(ybuf[:, g * HG_SET:(g + 1) * HG_SET, pair[d] * P:(pair[d] + 1) * P],
                                       ps[:, 2, :].rearrange("p (h t) -> p h t", h=HG_SET)).then_inc(o_done[d], 1)

            def ffn(layer):
                n0 = 12 + layer * 4 * FFN_H
                for half in range(2):
                    t0 = FIRST_OF[("gate", (layer, half * FFN_H))]
                    for i in range(2 * FFN_H):
                        t, n = t0 + i, n0 + half * 2 * FFN_H + i
                        prep(t)
                        conv_in(t, n)
                        if i % 2 == 0:
                            act.wait_ge(conv_ready, n + 1)
                            gi = (2 * layer + half) * FFN_H + i // 2
                            if gi:
                                act.wait_ge(g_ready, gi)
                            nc.scalar.activation(sq[:, 0, 0:CP], wk[:, 2 + n % 2, 0:CP], ACT.Silu).then_inc(conv_done, 1)
                    for m in range(KT):
                        t = t0 + 2 * FFN_H + m
                        prep(t)
                        if half == 0:
                            evac(t, ybuf[:, m])

            nt = lambda t: (tile_free[t % 2], t // 2 + 1)
            act.wait_ge(small_in, 48)
            nc.scalar.activation(condT[:].rearrange("p k c -> p (k c)"), par("cond"), ACT.Silu).then_inc(cond_ready, 1)
            nc.scalar.activation(eal[:], par("a_log"), ACT.Exp).then_inc(lb_e, 1)
            act.wait_ge(lb_d, 1)
            nc.scalar.activation(lbt[:, 1], lbt[:, 0], ACT.Exp).then_inc(lb_e, 1)
            squares(N_ADALN0, lambda i: xT[:, i], lambda i: act.wait_ge(x_in, 16) if i == 0 else None)
            root(N_ADALN0, D_MODEL)
            affine(0, 0, 0, 0)
            t = n = 0
            for g in range(SSD_GROUPS):
                if g == 0:
                    prep(t)
                    act.wait_ge(dt_abs, 1)
                    link(nc.scalar.activation(dtw[:, 2], dtw[:, 1], ACT.Exp, scale=-1.0))
                    nc.scalar.activation(dtw[:, 1], dtw[:, 2], ACT.Ln, bias=1.0).then_inc(dt_log, 1)
                    t += 1
                for i in range(6):
                    prep(t)
                    conv_in(t, n)
                    act.wait_ge(conv_ready, n + 1)
                    dst = bcT[:, i] if i < 2 else xsT[:, i - 2]
                    if n == 6:
                        act.wait_ge(yu_done, len(SSD_UNITS))
                    a, b = conv_cols(wk[:, 2 + n % 2])
                    nc.scalar.activation(dst[:, 0:SAMPLE], a, ACT.Silu)
                    nc.scalar.activation(dst[:, SAMPLE:NT], b, ACT.Silu).then_inc(conv_done, 1)
                    t += 1
                    n += 1
                for i in range(4):
                    prep(t)
                    if g and i == 0:
                        act.wait_ge(yz_ready, 1)
                    evac(t, zs[:, i], ACT.Silu)
                    t += 1
                ssd(g)
            for g in range(2):
                if g == 0:
                    act.wait_ge(yz_ready, 2)
                    act.wait_ge(sfin_out, 64)
                for i in range(4):
                    prep(t)
                    evac(t, qs[:, i], ACT.Silu)
                    t += 1
                if g:
                    act.wait_ge(kk_ready, 2 * LEVELS * len(HG_PAIRS))
                for d in range(2):
                    for i in range(4):
                        prep(t)
                        arrived(t)
                        nc.scalar.activation(fg[:, d, i], pg[:, t % 2, 0:NT], ACT.Sigmoid)
                        nc.scalar.activation(kg[:, d, i], pg[:, t % 2, 0:NT], ACT.Sigmoid,
                                             scale=-1.0).then_inc(tile_free[t % 2], 1)
                        t += 1
                for i in range(4):
                    prep(t)
                    arrived(t)
                    nc.scalar.copy(vtok[:, :, i * P:(i + 1) * P],
                                   pg[:, t % 2, 0:NT].rearrange("p (t n) -> p t n", t=TT)).then_inc(tile_free[t % 2], 1)
                    t += 1
                hgrn(g)
            act.wait_ge(o_done[0], 10)
            act.wait_ge(o_done[1], 10)
            for h in range(KT):
                prep(t)
                squares(N_HG + h, lambda i, h=h: ybuf[:, h], lambda i: None)
                if h >= 2:
                    act.wait_ge(og_done, h - 1)
                evac(t, wk[:, h % 2, 0:NT], ACT.Silu)
                root(N_HG + h, P)
                t += 1
            for m in range(KT):
                prep(t)
                if m == 0:
                    act.wait_ge(h_ready, H_BASE["hg"] + KT)
                evac(t, ybuf[:, m])
                t += 1
            squares(N_SSD, lambda i: xT[:, i], lambda i: act.wait_ge(yssd_in, 16) if i == 0 else None)
            root(N_SSD, D_MODEL)
            for m in range(KT):
                prep(t)
                t += 1

            def y_squares(n, last_t):
                squares(n, lambda i: ybuf[:, i], lambda i: act.wait_ge(*nt(last_t + i)))
                root(n, D_MODEL)

            def x_squares(n, k):
                squares(n, lambda i: xT[:, i], lambda i: act.wait_ge(x_ready, KT * k + i + 1))
                root(n, D_MODEL)

            y_squares(N_RES0, FIRST_OF[("out", (0, 0))])
            x_squares(N_FFN0, 0)
            affine(1, 0, 1, H_BASE["ffn0"])
            ffn(0)
            y_squares(N_RES1, FIRST_OF[("down", (0, 1, 0))])
            x_squares(N_ATT, 1)
            affine(2, 1, 0, H_BASE["att"])
            t0 = FIRST_OF["aq"]
            for i in range(14):
                t = t0 + i
                prep(t)
                if i < 12:
                    dst = aq[:, i] if i < 8 else ak[:, i - 8, 0:NT]
                    evac(t, dst)
                    squares(N_QK + i, lambda _, dst=dst: dst, lambda _, t=t: act.wait_ge(*nt(t)))
                else:
                    act.wait_ge(tile_ready, t + 1)
                    nc.scalar.copy(av[:, 0:TT, (i - 12) * P:(i - 11) * P],
                                   pg[:, t % 2, 0:NT].rearrange("p (t n) -> p t n", t=TT)).then_inc(tile_free[t % 2], 1)
                if 1 <= i <= 12:
                    root(N_QK + i - 1, HD)
            tr_evac_k = (ak[:, :, NT:NT + P], kout[:])
            act.wait_ge(tr_ready, 15)
            nc.scalar.copy(tr_evac_k[0], ps[:, 0, :].rearrange("p (k t) -> p k t", k=KV_HEADS)).then_inc(tr_done, 1)
            act.wait_ge(tr_ready, 16)
            nc.scalar.copy(tr_evac_k[1], ps[:, 1, :].rearrange("p (k t) -> p k t", k=KV_HEADS)[:, :, 0:HD]).then_inc(tr_done, 1)
            prep(FIRST_OF["aout"] - 1)
            nu = len(ATT_UNITS)

            def att_exp(u):
                n = P if ATT_UNITS[u][1] == PROMPT_TT else NT
                act.wait_ge(mx_ready, u + 1)
                if u >= 2:
                    act.wait_ge(pt_ready, u - 1)
                nc.scalar.activation(pr[:, u % 2, 0:n], pg[:, u % 2, 0:n], ACT.Exp, scale=HD ** -0.5,
                                     bias=mxs[:, u % 2, 1:2], accum_out=mxs[:, u % 2, 2:3]).then_inc(pe_exp, 1)

            def att_pt(u):
                n = P if ATT_UNITS[u][1] == PROMPT_TT else NT
                act.wait_ge(pt_ready, u + 1)
                if u >= 2:
                    act.wait_ge(ao_ready, u - 1)
                nc.scalar.copy(pt[:, u % 2].rearrange("p t n -> p (t n)")[:, 0:n],
                               ps[:, 0:2, :].rearrange("p a b -> p (a b)")[:, 0:n]).then_inc(pt_done, 1)

            for u in range(nu + 1):
                if u < nu:
                    att_exp(u)
                if u >= 1:
                    att_pt(u - 1)
            for m in range(KT):
                prep(FIRST_OF["aout"] + m)
            y_squares(N_RES2, FIRST_OF["aout"])
            x_squares(N_FFN1, 2)
            affine(3, 1, 1, H_BASE["ffn1"])
            ffn(1)
            y_squares(N_RES3, FIRST_OF[("down", (1, 1, 0))])
            for ft in range(KT):
                act.wait_ge(x_ready, 3 * KT + ft + 1)
                act.dma_start(y_out[:, ft], xT[:, ft]).then_inc(y_written, 16)
            act.wait_ge(y_written, 16 * KT)

        @block.vector
        def _(dve):
            chain = [0]
            prepped = [0]
            V = nc.vector

            def link(ins):
                chain[0] += 1
                ins.then_inc(vch, 1)
                dve.wait_ge(vch, chain[0])

            def prep(t):
                upto = min(TILES[t][2][-1][0] + 2, N_SLOTS)
                for s in range(prepped[0], upto):
                    dve.wait_ge(whi_ready, s + 1)
                    V.tensor_tensor(wlo[:, s % 2], ring[:, s % RING], whi[:, s % 2].bitcast(F32),
                                    ALU.subtract).then_inc(wlo_ready, 1)
                prepped[0] = max(prepped[0], upto)

            def arrived(t):
                dve.wait_ge(tile_ready, t + 1)
                a = ada_after(t)
                if a is not None:
                    V.tensor_scalar(mod[:, a, :], pada(a), par("ada_b", a), None, ALU.add)

            def ada(a):
                dve.wait_ge(ada_ready, a + 1)
                V.tensor_scalar(mod[:, a, :], pada(a), par("ada_b", a), None, ALU.add).then_inc(mod_ready, 1)

            def recip(n):
                dve.wait_ge(rt_ready, n + 1)
                ins = V.reciprocal(rb[:], rt[:])
                ins.then_inc(r_ready, 1)
                dve.wait_ge(r_ready, n + 1)

            def split(dst, src, n):
                link(V.tensor_copy(dst[0], src))
                V.tensor_tensor(dst[1], src, dst[0].bitcast(F32), ALU.subtract).then_inc(h_ready, 1)

            def adaln(k, layer, which, base, n):
                modulated(dve, (layer * 6 + 3 * which + 2) * KT)
                i = (layer * 6 + 3 * which + 1) * KT
                gcol = (layer * 4 + 2 * which) * KT
                g = par("norm_g", gcol, gcol + KT).unsqueeze(2).broadcast_to([P, KT, 2])
                link(V.scalar_tensor_tensor(out=scal[:, 0], in0=mod[:, i:i + KT, :], scalar=1.0, in1=g,
                                            op0=ALU.add, op1=ALU.mult))
                recip(n)
                for ft in range(KT + 1):
                    if ft < KT:
                        if ft >= 2:
                            dve.wait_ge(aff_ready, k * KT + ft - 1)
                        V.tensor_tensor(wk[:, ft % 2, 0:NT], xT[:, ft], rb[:], ALU.mult).then_inc(t_ready, 1)
                    if ft:
                        f = ft - 1
                        dve.wait_ge(aff_ready, k * KT + f + 1)
                        split((hh[:, f], hl[:, f]), wk[:, 2 + f % 2, 0:NT], base + f)

            def residual(k, layer, which, n):
                i = (layer * 6 + 3 * which + 2) * KT
                modulated(dve, i + KT)
                gcol = (layer * 4 + 2 * which + 1) * KT
                g = par("norm_g", gcol, gcol + KT).unsqueeze(2).broadcast_to([P, KT, 2])
                link(V.tensor_tensor(scal[:, 1], mod[:, i:i + KT, :], g, ALU.mult))
                recip(n)
                if k == 0:
                    dve.wait_ge(x_again, 16)
                for ft in range(KT):
                    link(V.tensor_tensor(ybuf[:, ft], ybuf[:, ft], rb[:], ALU.mult))
                    for lo, hi, c in SEQS:
                        last = V.scalar_tensor_tensor(out=xT[:, ft, lo:hi], in0=ybuf[:, ft, lo:hi],
                                                      scalar=scal[:, 1, ft, c:c + 1], in1=xT[:, ft, lo:hi],
                                                      op0=ALU.mult, op1=ALU.add)
                    last.then_inc(x_ready, 1)

            def pads():
                for c in (0, SAMPLE + 1, UP - 1):
                    last = V.memset(wk[:, 0:2, c:c + 1], 0.0)
                link(last)

            def conv(t, n, w, b):
                dve.wait_ge(tile_free[t % 2], t // 2 + 1)
                u, c = wk[:, n % 2], wk[:, 2 + n % 2, 0:CP]
                link(V.tensor_scalar(c, u[:, 1:CP + 1], w[1], b, ALU.mult, ALU.add))
                link(V.scalar_tensor_tensor(out=c, in0=u[:, 0:CP], scalar=w[0], in1=c, op0=ALU.mult, op1=ALU.add))
                ins = V.scalar_tensor_tensor(out=c, in0=u[:, 2:CP + 2], scalar=w[2], in1=c, op0=ALU.mult, op1=ALU.add)
                ins.then_inc(conv_ready, 1)

            def per_head(a, n):
                return a.unsqueeze(2).broadcast_to([P, a.shape[1], n])

            def ssd(g):
                ns = len(SSD_STATES)
                hs = lambda d: slice(d * 16 + HPG * g, d * 16 + HPG * (g + 1))
                dve.wait_ge(dexp_ready, g + 1)
                for d in range(2):
                    last = V.tensor_tensor(wdec[:, d], dtt[:, :, hs(d)], dect[:, 2 * d], ALU.mult)
                link(last)
                dve.wait_ge(tr_done, 7 * (g + 1))
                dve.wait_ge(s0_in, 16 * 2 * (g + 1))
                for i, (d, t) in enumerate(SSD_STATES):
                    n = g * ns + i
                    if n:
                        dve.wait_ge(ls_ready, n)
                    V.tensor_tensor(xw.rearrange("p (h n) -> p h n", h=HPG),
                                    xtok[:, t].rearrange("p (h n) -> p h n", h=HPG),
                                    per_head(wdec[:, d, t], SSD_P), ALU.mult).then_inc(xw_ready, 1)
                    if t == PROMPT_TT:
                        dve.wait_ge(ls_ready, n + 1)
                        if 2 * g + d:
                            dve.wait_ge(sfin_out, 16 * (2 * g + d))
                        V.tensor_copy(sfin, ps[:, 3, :]).then_inc(st_ready, 1)
                        continue
                    nxt = t + 1 if d == 0 else t - 1
                    view = lambda a: a.rearrange("p (h n) -> p h n", h=HPG)
                    link(V.tensor_tensor(view(st[:, d, nxt]), view(st[:, d, t]),
                                         per_head(dect[:, 2 * d + 1, t], SSD_P), ALU.mult))
                    dve.wait_ge(ls_ready, n + 1)
                    V.tensor_tensor(st[:, d, nxt], st[:, d, nxt], ps[:, 3, :], ALU.add).then_inc(st_ready, 1)
                    dve.wait_ge(st_ready, n + 1)
                dve.wait_ge(yd_ready, g + 1)
                for i, (t, q) in enumerate(SSD_UNITS):
                    u = g * len(SSD_UNITS) + i
                    tok = slice(t * P, (t + 1) * P)
                    heads = lambda d: slice(d * 16 + HPG * g + 4 * q, d * 16 + HPG * g + 4 * q + 4)
                    for d in range(2):
                        if u:
                            dve.wait_ge(dd_ready, 2 * u)
                        V.tensor_tensor(ra[:, d], per_head(adt[:, t, heads(d)], P),
                                        cm[:, (LE, GE)[d], :].unsqueeze(1).broadcast_to([P, 4, P]),
                                        ALU.mult).then_inc(ra_ready, 1)
                    if q == 0:
                        dve.wait_ge(cb_ready, u // 2 + 1)
                        if u:
                            dve.wait_ge(yu_ready, u)
                        for d in range(2):
                            V.tensor_tensor(cbm[:, d], ps[:, 2, 0:P], cm[:, (LE, GE)[d], :], ALU.mult)
                            link(V.tensor_tensor(xd[:, d].rearrange("p (h n) -> p h n", h=HPG),
                                                 xtok[:, t].rearrange("p (h n) -> p h n", h=HPG),
                                                 per_head(dtt[:, t, hs(d)], SSD_P), ALU.mult))
                    for d in range(2):
                        dve.wait_ge(ex_ready, 2 * u + d + 1)
                        V.tensor_tensor(eg[:, d], eg[:, d], cbm[:, d].unsqueeze(1).broadcast_to([P, 4, P]),
                                        ALU.mult).then_inc(g_done, 1)
                    dve.wait_ge(yu_ready, u + 1)
                    y = ybuf[:, 4 * g + 2 * q:4 * g + 2 * q + 2, tok]
                    V.tensor_tensor(y, y, ps[:, 3, 0:2 * P].rearrange("p (f t) -> p f t", f=2),
                                    ALU.add).then_inc(yu_done, 1)
                dve.wait_ge(yu_done, (g + 1) * len(SSD_UNITS))
                V.tensor_tensor(ybuf[:, 4 * g:4 * g + 4], ybuf[:, 4 * g:4 * g + 4], zs[:], ALU.mult).then_inc(yz_ready, 1)

            def hgrn(g):
                for p, pair in enumerate(HG_PAIRS):
                    np_ = g * len(HG_PAIRS) + p
                    tok = [slice(t * P, (t + 1) * P) for t in pair]
                    for d in range(2):
                        if np_:
                            dve.wait_ge(o_ready, 2 * np_)
                        V.tensor_tensor(qp[:, d], qs[:, :, tok[d]], fg[:, d, :, tok[d]],
                                        ALU.mult).then_inc(qp_ready, 1)
                        dve.wait_ge(dg_ready, 2 * np_ + d + 1)
                        V.copy_predicated(att[:, d], m8[:, 2 * LEVELS * 64:].unsqueeze(1).broadcast_to([P, HG_SET, P]),
                                          pg[:, 0, d * 512:(d + 1) * 512]
                                          .rearrange("p (h t) -> p h t", h=HG_SET)).then_inc(qp_ready, 1)
                    for i in range(LEVELS):
                        w = 1 << i
                        for d in range(2):
                            n = (np_ * LEVELS + i) * 2 + d
                            dve.wait_ge(lv_ready, n + 1)
                            mo = (d * LEVELS + i) * 64
                            mask = m8[:, mo:mo + 64].rearrange("p (b w) -> p b w", w=w).unsqueeze(1)
                            V.copy_predicated(halves(att[:, d], w, 1 - d), mask.broadcast_to([P, HG_SET, 64 // w, w]),
                                              ps[:, d, 0:256]
                                              .rearrange("p (h b w) -> p h b w", h=HG_SET, w=w))
                            tot = fg[:, d, :, tok[d]] if i == 0 else tlevel(d, i)
                            pairs = tot.rearrange("p h (b t) -> p h b t", t=2)
                            V.tensor_tensor(tlevel(d, i + 1), pairs[:, :, :, 0], pairs[:, :, :, 1], ALU.mult)
                            q = halves(qp[:, d], w, 1 - d)
                            V.tensor_tensor(q, q, pairs[:, :, :, d].unsqueeze(3)
                                            .broadcast_to([P, HG_SET, 64 // w, w]), ALU.mult).then_inc(qp_ready, 1)
                    for d in range(2):
                        v = 2 * np_ + d
                        if p in (1, 2) or (p == 0 and d == 0):
                            continue
                        dve.wait_ge(o_ready, v + 1)
                        dve.wait_ge(o_done[0], np_ if d == 0 else np_ + 1) if (d or np_) else None
                        dve.wait_ge(o_done[1], np_) if np_ else None
                        o = ybuf[:, g * HG_SET:(g + 1) * HG_SET, tok[d]]
                        V.tensor_tensor(o, o, ps[:, 2, :].rearrange("p (h t) -> p h t", h=HG_SET),
                                        ALU.add).then_inc(o_done[d], 1)
                    if p < len(HG_PAIRS) - 1:
                        for d in range(2):
                            v = 2 * (np_ - g) + d
                            dve.wait_ge(hs_ready, v + 1)
                            src = ps[:, 3, :].rearrange("p (h t) -> p h t", h=HG_SET)
                            if p == 0:
                                if g:
                                    dve.wait_ge(hfin_out, 32)
                                V.tensor_copy(hfin[:, d], src).then_inc(hs_done, 1)
                                continue
                            dve.wait_ge(hst_in, 16 * (g + 1))
                            for h in range(HG_SET):
                                last = V.scalar_tensor_tensor(out=hst[:, d, h], in0=hst[:, d, h],
                                                              scalar=tlevel(d, LEVELS)[:, h], in1=src[:, h],
                                                              op0=ALU.mult, op1=ALU.add)
                            last.then_inc(hs_done, 1)

            def ffn(layer):
                n0 = 12 + layer * 4 * FFN_H
                fw = lambda tap, i: par("fconv_w", (layer * 3 + tap) * 44 + i)
                pads()
                if layer:
                    dve.wait_ge(kv_out, 32)
                for half in range(2):
                    t0 = FIRST_OF[("gate", (layer, half * FFN_H))]
                    for i in range(2 * FFN_H):
                        t, n = t0 + i, n0 + half * 2 * FFN_H + i
                        prep(t)
                        feat = half * FFN_H + i // 2 + (i % 2) * FFN_T
                        conv(t, n, [fw(k, feat) for k in range(3)], par("fconv_b", layer * 44 + feat))
                        if i % 2:
                            gi = i // 2
                            gn = (2 * layer + half) * FFN_H + gi
                            dve.wait_ge(conv_ready, n + 1)
                            dve.wait_ge(conv_done, 12 + gn + 1)
                            if half and gi == 0:
                                dve.wait_ge(tile_ready, t0)
                            link(V.tensor_tensor(sq[:, 1, 0:CP], wk[:, 2 + n % 2, 0:CP], sq[:, 0, 0:CP], ALU.mult))
                            link(V.tensor_copy(gh[:, gi, 0:CP], sq[:, 1, 0:CP]))
                            V.tensor_tensor(gl[:, gi, 0:CP], sq[:, 1, 0:CP], gh[:, gi, 0:CP].bitcast(F32),
                                            ALU.subtract).then_inc(g_ready, 1)
                    for m in range(KT):
                        t = t0 + 2 * FFN_H + m
                        prep(t)
                        if half:
                            arrived(t)
                            V.tensor_tensor(ybuf[:, m], ybuf[:, m], pg[:, t % 2, 0:NT],
                                            ALU.add).then_inc(tile_free[t % 2], 1)

            dve.wait_ge(small_in, 48)
            link(V.tensor_copy(m8[:], mask_in))
            V.tensor_tensor(lbt[:, 0], par("lb"), par("lb"), ALU.subtract).then_inc(lb_d, 1)
            dve.wait_ge(lb_e, 2)
            link(V.reciprocal(lbt[:, 2], lbt[:, 1]))
            link(V.tensor_tensor(lbt[:, 3], lbt[:, 1], lbt[:, 2], ALU.mult))
            link(V.tensor_tensor(lbt[:, 0], lbt[:, 3], lbt[:, 3], ALU.subtract))
            link(V.tensor_scalar(lbt[:, 1], lbt[:, 0], -1.0, 1.0, ALU.mult, ALU.add))
            for a in range(ADA_FIRST):
                ada(a)
            adaln(0, 0, 0, 0, N_ADALN0)
            pads()
            t = n = 0
            for g in range(SSD_GROUPS):
                if g == 0:
                    prep(t)
                    arrived(t)
                    raw = pg[:, 0, 0:NT].rearrange("p (t n) -> p t n", t=TT)[:, :, 0:32]
                    V.tensor_tensor(dtw[:, 0], raw, par("dt_b").unsqueeze(1).broadcast_to([P, TT, 32]),
                                    ALU.add).then_inc(tile_free[0], 1)
                    dve.wait_ge(tile_free[0], 1)
                    V.scalar_tensor_tensor(out=dtw[:, 1], in0=dtw[:, 0], scalar=-1.0, in1=dtw[:, 0],
                                           op0=ALU.mult, op1=ALU.max).then_inc(dt_abs, 1)
                    dve.wait_ge(dt_log, 1)
                    link(V.scalar_tensor_tensor(out=dtt[:], in0=dtw[:, 0], scalar=0.0, in1=dtw[:, 1],
                                                op0=ALU.max, op1=ALU.add))
                    V.scalar_tensor_tensor(out=adt[:], in0=dtt[:], scalar=-1.0,
                                           in1=eal[:].unsqueeze(1).broadcast_to([P, TT, 32]),
                                           op0=ALU.mult, op1=ALU.mult).then_inc(dt_ready, 1)
                    dve.wait_ge(dt_ready, 1)
                    t += 1
                for i in range(6):
                    prep(t)
                    feat = TILES[t][1]
                    if n >= 2:
                        dve.wait_ge(conv_done, n - 1)
                    conv(t, n, [par("sconv_w", k * 12 + feat) for k in range(3)], par("sconv_b", feat))
                    t += 1
                    n += 1
                for i in range(4):
                    prep(t)
                    t += 1
                for b in range(2):
                    dve.wait_ge(tile_free[b], freed(b, t))
                ssd(g)
            dve.wait_ge(sfin_out, 64)
            dve.wait_ge(yz_ready, 2)
            V.memset(att[:], 0.0).then_inc(att_zero, 1)
            dve.wait_ge(att_zero, 1)
            for g in range(2):
                for i in range(4):
                    prep(t)
                    t += 1
                for d in range(2):
                    for i in range(4):
                        prep(t)
                        dve.wait_ge(tile_free[t % 2], t // 2 + 1)
                        c = d * KT + g * HG_SET + i
                        link(V.tensor_scalar(fg[:, d, i], fg[:, d, i], lbt[:, 1, c:c + 1], lbt[:, 0, c:c + 1],
                                             ALU.mult, ALU.add))
                        V.tensor_scalar(fg[:, d, i], fg[:, d, i], F_FLOOR, None, ALU.max)
                        V.tensor_scalar(kg[:, d, i], kg[:, d, i], lbt[:, 1, c:c + 1], None,
                                        ALU.mult).then_inc(fk_ready, 1)
                        t += 1
                for i in range(4):
                    prep(t)
                    t += 1
                dve.wait_ge(fk_ready, 8 * (g + 1))
                hgrn(g)
            for h in range(KT):
                prep(t)
                recip(N_HG + h)
                dve.wait_ge(tile_free[t % 2], t // 2 + 1)
                link(V.tensor_tensor(ybuf[:, h], ybuf[:, h], rb[:], ALU.mult))
                V.scalar_tensor_tensor(out=ybuf[:, h], in0=ybuf[:, h], scalar=par("hg_g", h), in1=wk[:, h % 2, 0:NT],
                                       op0=ALU.mult, op1=ALU.mult).then_inc(og_done, 1)
                t += 1
            dve.wait_ge(tile_ready, t)
            dve.wait_ge(og_done, KT)
            for f in range(KT):
                split((hh[:, f], hl[:, f]), ybuf[:, f], H_BASE["hg"] + f)
            for m in range(KT):
                prep(t)
                t += 1
            recip(N_SSD)
            dve.wait_ge(tile_ready, t)
            for f in range(KT):
                link(V.tensor_tensor(xT[:, f], xT[:, f], rb[:], ALU.mult))
                link(V.tensor_scalar(xT[:, f], xT[:, f], par("ssd_g", f), None, ALU.mult))
                split((hh[:, f], hl[:, f]), xT[:, f], H_BASE["ssd"] + f)
            for m in range(KT):
                prep(t)
                arrived(t)
                if m == 0:
                    for b in range(2):
                        dve.wait_ge(tile_free[b], freed(b, t))
                V.tensor_tensor(ybuf[:, m], ybuf[:, m], pg[:, t % 2, 0:NT], ALU.add).then_inc(tile_free[t % 2], 1)
                t += 1
            for b in range(2):
                dve.wait_ge(tile_free[b], freed(b, t))
            residual(0, 0, 0, N_RES0)
            adaln(1, 0, 1, H_BASE["ffn0"], N_FFN0)
            ffn(0)
            for b in range(2):
                dve.wait_ge(tile_free[b], freed(b, FIRST_OF["aq"]))
            residual(1, 0, 1, N_RES1)
            adaln(2, 1, 0, H_BASE["att"], N_ATT)
            t0 = FIRST_OF["aq"]

            def qk_finish(j):
                buf = aq[:, j] if j < 8 else ak[:, j - 8, 0:NT]
                recip(N_QK + j)
                link(V.tensor_tensor(buf, buf, rb[:], ALU.mult))
                V.tensor_scalar(buf, buf, par("q_g") if j < 8 else par("k_g"), None, ALU.mult).then_inc(qk_norm, 1)

            def rope_apply(j):
                buf = aq[:, j, 0:SAMPLE] if j < 8 else ak[:, j - 8, 0:SAMPLE]
                dve.wait_ge(rot_ready, j + 1)
                if j == 0:
                    dve.wait_ge(kv_in, 16 * 5)
                V.tensor_tensor(wk[:, 0, 0:SAMPLE], ps[:, 1, :], cs[:, 1], ALU.mult)
                link(V.tensor_tensor(buf, buf, cs[:, 0], ALU.mult))
                V.tensor_tensor(buf, buf, wk[:, 0, 0:SAMPLE], ALU.add).then_inc(rope_done, 1)

            for i in range(14):
                prep(t0 + i)
                if 1 <= i <= 12:
                    qk_finish(i - 1)
                if i >= 2:
                    rope_apply(i - 2)
            dve.wait_ge(tr_done, 16)
            prep(FIRST_OF["aout"] - 1)
            nu = len(ATT_UNITS)

            def att_max(u):
                n = P if ATT_UNITS[u][1] == PROMPT_TT else NT
                dve.wait_ge(sc_ready, u + 1)
                link(V.reduce_max(mxs[:, u % 2, 0:1], pg[:, u % 2, 0:n], AX_X))
                V.tensor_scalar(mxs[:, u % 2, 1:2], mxs[:, u % 2, 0:1], -HD ** -0.5, None, ALU.mult).then_inc(mx_ready, 1)

            def att_prob(u):
                n = P if ATT_UNITS[u][1] == PROMPT_TT else NT
                dve.wait_ge(pe_exp, u + 1)
                link(V.reciprocal(mxs[:, u % 2, 3:4], mxs[:, u % 2, 2:3]))
                V.tensor_scalar(pr[:, u % 2, 0:n], pr[:, u % 2, 0:n], mxs[:, u % 2, 3:4], None,
                                ALU.mult).then_inc(pr_ready, 1)

            def att_evac(u):
                h, b = ATT_UNITS[u]
                r = HD * (h % 2)
                dve.wait_ge(ao_ready, u + 1)
                V.tensor_copy(ybuf[r:r + HD, h // 2, b * P:(b + 1) * P],
                              ps[r:r + HD, 2 + u % 2, 0:P]).then_inc(ao_done, 1)

            for u in range(nu + 3):
                if u < nu:
                    att_max(u)
                if 1 <= u <= nu:
                    att_prob(u - 1)
                if u >= 3:
                    att_evac(u - 3)
            dve.wait_ge(ao_done, nu)
            for f in range(KT):
                split((hh[:, f], hl[:, f]), ybuf[:, f], H_BASE["ao"] + f)
            for m in range(KT):
                t = FIRST_OF["aout"] + m
                prep(t)
                dve.wait_ge(tile_ready, t + 1)
                if m == 0:
                    dve.wait_ge(h_ready, H_BASE["ao"] + KT)
                V.tensor_copy(ybuf[:, m], pg[:, t % 2, 0:NT]).then_inc(tile_free[t % 2], 1)
            t = FIRST_OF["aout"] + KT
            for b in range(2):
                dve.wait_ge(tile_free[b], freed(b, t))
            residual(2, 1, 0, N_RES2)
            adaln(3, 1, 1, H_BASE["ffn1"], N_FFN1)
            ffn(1)
            for b in range(2):
                dve.wait_ge(tile_free[b], freed(b, len(TILES)))
            residual(3, 1, 1, N_RES3)

        @block.gpsimd
        def _(pool):
            G = nc.gpsimd
            for g in range(SSD_GROUPS):
                if g:
                    pool.wait_ge(yu_done, len(SSD_UNITS))
                else:
                    pool.wait_ge(h_ready, KT)
                for d in range(2):
                    G.dma_start(st[:, d, 0 if d == 0 else 3], s_ssd[:, d, 512 * g:512 * (g + 1)]).then_inc(s0_in, 16)
                for d in range(2):
                    pool.wait_ge(st_ready, g * len(SSD_STATES) + d + 1)
                    G.dma_start(ssd_out[:, d, 512 * g:512 * (g + 1)], sfin).then_inc(sfin_out, 16)
                for i, (t, q) in enumerate(SSD_UNITS):
                    u = g * len(SSD_UNITS) + i
                    for d in range(2):
                        pool.wait_ge(exc_ready, 2 * u + d + 1)
                        G.tensor_tensor(ec[:, d], ec[:, d],
                                        bcT[:, 1, t * P:(t + 1) * P].unsqueeze(1).broadcast_to([P, 4, P]),
                                        ALU.mult).then_inc(cs_ready, 1)
                pool.wait_ge(yz_ready, g + 1)
                G.dma_start(yssd_dram[:, 4 * NT * g:4 * NT * (g + 1)].rearrange("p (f t) -> p f t", f=4),
                            ybuf[:, 4 * g:4 * g + 4]).then_inc(yssd_out, 16)
            pool.wait_ge(sfin_out, 64)
            for g in range(2):
                if g:
                    pool.wait_ge(o_ready, 10)
                    pool.wait_ge(hs_done, 8)
                G.dma_start(hst[:], s_hg[:, :, g * HG_SET:(g + 1) * HG_SET]).then_inc(hst_in, 16)
                for p, pair in enumerate(HG_PAIRS):
                    np_ = g * len(HG_PAIRS) + p
                    for i in range(LEVELS):
                        w = 1 << i
                        for d in range(2):
                            n = (np_ * LEVELS + i) * 2 + d
                            tok = slice(pair[d] * P, (pair[d] + 1) * P)
                            pool.wait_ge(lv_ready, n + 1)
                            tot = fg[:, d, :, tok] if i == 0 else tlevel(d, i)
                            tot = tot.rearrange("p h (b t) -> p h b t", t=2)[:, :, :, 1 - d]
                            k = halves(kg[:, d, :, tok], w, d)
                            G.tensor_tensor(k, k, tot.unsqueeze(3).broadcast_to([P, HG_SET, 64 // w, w]),
                                            ALU.mult).then_inc(kk_ready, 1)
                    if p == 0:
                        pool.wait_ge(hs_done, 8 * g + 2)
                        for d in range(2):
                            G.dma_start(hg_out[:, d, g * HG_SET:(g + 1) * HG_SET], hfin[:, d]).then_inc(hfin_out, 16)
            pool.wait_ge(o_done[0], 10)
            pool.wait_ge(o_done[1], 10)
            pool.wait_ge(hs_done, 16)
            pool.wait_ge(kk_ready, 4 * LEVELS * len(HG_PAIRS))
            pool.wait_ge(hfin_out, 64)
            pool.wait_ge(yssd_out, 32)
            G.dma_start(xT[:].rearrange("p f t -> p (f t)"), yssd_dram).then_inc(yssd_in, 16)
            pool.wait_ge(h_ready, H_BASE["ssd"] + KT)
            G.dma_start(xT[:], x).then_inc(x_again, 16)
            pool.wait_ge(tile_ready, FIRST_OF["aq"])
            for a in range(2):
                G.dma_start(ck[:, :, a], cache_k).then_inc(kv_in, 16)
            G.dma_start(av[:, TT].rearrange("p (k n) -> p k n", k=KV_HEADS), cache_v).then_inc(kv_in, 16)
            G.dma_start(cs[:, 0], rope[:, 0]).then_inc(kv_in, 16)
            G.dma_start(cs[:, 1], rope[:, 1]).then_inc(kv_in, 16)
            pool.wait_ge(tr_done, 16)
            G.dma_start(k_out, kout[:]).then_inc(kv_out, 16)
            for b in range(2):
                pool.wait_ge(tile_free[b], freed(b, FIRST_OF["aout"]))
            G.dma_start(v_out, av[:, PROMPT_TT].rearrange("p (k n) -> p k n", k=KV_HEADS)).then_inc(kv_out, 16)
            pool.wait_ge(kv_out, 32)


H_BASE = {"adaln0": 0, "hg": 8, "ssd": 16, "ffn0": 24, "att": 32, "ao": 40, "ffn1": 48}


def freed(b, t):
    return (t + 1 - b) // 2


def qp_need(np_, i, d):
    base = np_ * (4 + 2 * LEVELS)
    return base + 4 if i == 0 else base + 4 + 2 * (i - 1) + d + 1


def constant_arrays():
    j, s = np.arange(P)[:, None], np.arange(P)[None, :]
    rot = np.zeros((P, P), np.float32)
    for m in range(P):
        if m % 32 < 16:
            rot[m + 16, m] = -1.0
        else:
            rot[m - 16, m] = 1.0
    mats = [j == s, j >= 0 * s, j > s, j < s, j <= s, j >= s, j // 64 == s // 64]
    cm = np.stack([a.astype(np.float32) for a in mats] + [rot], axis=1)
    m8 = []
    t = np.arange(P)
    for d in range(2):
        for i in range(LEVELS):
            w = 1 << i
            late = t.reshape(-1, 2, w)[:, 1 - d].reshape(-1)
            same = (t[:, None] // (2 * w)) == (late[None, :] // (2 * w))
            other = (t[:, None] // w) % 2 == d
            m8.append(same & other)
    m8.append(j == s)
    m8 = np.concatenate(m8, axis=1).astype(np.float32)
    nf = HD // 4
    inv = np.float32(10000.0) ** (-np.arange(nf, dtype=np.float32) / np.float32(nf))
    tok = np.arange(SAMPLE)
    pos = np.stack([tok // 64, tok % 64]).astype(np.float32)
    p = np.arange(P) % HD
    ang = (pos[p // 32] * inv[p % 16][:, None]).astype(np.float32)
    rope = np.stack([np.cos(ang), np.sin(ang)], axis=1).astype(np.float32)
    return np.ascontiguousarray(cm), np.ascontiguousarray(m8), np.ascontiguousarray(rope)


def feat(a):
    a = np.asarray(a)
    return a.reshape(-1, P).T


def wtiles(w):
    return w.reshape(KT, P, -1, P).transpose(2, 1, 0, 3)


def kernel(**inputs):
    import concourse.bacc as bacc
    from concourse.bass_utils import run_bass_kernel_spmd

    v = {k: np.asarray(a) for k, a in inputs.items()}
    cm, m8, rope = constant_arrays()

    def rows(a):
        return np.broadcast_to(a.reshape(1, -1), (P, a.size))

    cond = np.stack([v["c_ctx"].reshape(KT, P).T, v["c"].reshape(KT, P).T], axis=2).reshape(P, -1)
    small = np.concatenate([
        cond, feat(v["ada_b"]), feat(v["norm_g"]), feat(v["ssd_conv_w"]), feat(v["ssd_conv_b"]),
        feat(v["ffn_conv_w"]), feat(v["ffn_conv_b"]), feat(v["ssd_norm_g"]), feat(v["hg_norm_g"]),
        feat(np.repeat(v["ssd_d"].reshape(-1), SSD_P)), feat(v["hg_lb_logits"]),
        feat(np.tile(v["attn_q_norm"].reshape(-1), 2)), feat(np.tile(v["attn_k_norm"].reshape(-1), 2)),
        rows(v["ssd_dt_bias"]), rows(v["ssd_a_log"])], axis=1)

    w_in = v["ssm_w_in"][0]
    z0, x0, dt0 = 0, 1024, 2560
    q0, f0, v0, o0 = 2592, 3616, 5664, 6688
    w_out = v["ssm_w_out"][0]
    w_qkv = v["attn_w_qkv"][0]

    def w_of(kind, i):
        col = lambda a, n: a[:, n:n + P]
        if kind == "dt":
            return np.concatenate([w_in[:, dt0:dt0 + 32], np.zeros((D_MODEL, P - 32), np.float32)], axis=1)
        if kind in ("conv", "z", "q", "v", "og"):
            return col(w_in, {"conv": x0, "z": z0, "q": q0, "v": v0, "og": o0}[kind] + P * i)
        if kind == "zf":
            return col(w_in, f0 + D_MODEL * i[0] + P * i[1])
        if kind == "out":
            return col(w_out[D_MODEL * i[0]:D_MODEL * (i[0] + 1)], P * i[1])
        if kind in ("gate", "val"):
            return col(v["ffn_w_up"][i[0]], P * (i[1] + (FFN_T if kind == "val" else 0)))
        if kind == "aq":
            return col(w_qkv, P * i)
        if kind == "ak":
            k = w_qkv[:, D_MODEL + HD * i:D_MODEL + HD * (i + 1)]
            return np.concatenate([k, k], axis=1)
        if kind == "av":
            return col(w_qkv, D_MODEL + KV_HEADS * HD + P * i)
        return col(v["attn_w_out"][0], P * i)

    stream = np.zeros((N_SLOTS, P, KT, P), np.float32)
    for kind, i, kts in TILES:
        if kind == "down":
            w = v["ffn_w_down"][i[0]][i[1] * FFN_H * P:(i[1] + 1) * FFN_H * P, P * i[2]:P * (i[2] + 1)]
            for s, pos, k in kts:
                stream[s, :, pos] = w[k * P:(k + 1) * P]
        else:
            stream[kts[0][0]] = wtiles(w_of(kind, i))[0]
    wada = np.concatenate([wtiles(v["ada_w"][0]), wtiles(v["ada_w"][1])])

    tokens = np.concatenate([v["x_sample"][0], v["x_prompt"][0]], axis=0)
    arrays = {
        "x": tokens.T.reshape(KT, P, NT).transpose(1, 0, 2),
        "small_params": small,
        "consts": cm,
        "masks8": m8,
        "rope": rope,
        "s_ssd": v["state_ssd"][0, 0].reshape(2, D_MODEL, P).transpose(2, 0, 1),
        "s_hg": v["state_hgrn"][0, 0].transpose(2, 0, 1, 3),
        "ck_in": v["cache_k"][0, 0].transpose(1, 0, 2),
        "cv_in": v["cache_v"][0, 0].transpose(1, 0, 2),
        "wstream": stream,
        "wada": wada,
    }
    outs = {"y": (P, KT, NT), "k_new": (P, KV_HEADS, HD), "v_new": (P, KV_HEADS, HD),
            "ssd_new": (P, 2, D_MODEL), "hg_new": (P, 2, HG_HEADS, P)}
    nc = bacc.Bacc("TRN2", target_bir_lowering=False, num_devices=1)
    args, data = [], {}
    for name, a in arrays.items():
        a = np.ascontiguousarray(a)
        data[f"in_{name}"] = a
        args.append(nc.dram_tensor(f"in_{name}", a.shape, mybir.dt.from_np(a.dtype), kind="ExternalInput").ap())
    for name, shape in outs.items():
        args.append(nc.dram_tensor(f"out_{name}", shape, F32, kind="ExternalOutput").ap())
    hybrid_step(nc, *args)
    r = run_bass_kernel_spmd(nc, [data], core_ids=[0]).results[0]
    y = r["out_y"].transpose(1, 0, 2).reshape(D_MODEL, NT).T
    kv = lambda a: np.ascontiguousarray(a.transpose(1, 0, 2))[None, None]
    return (np.ascontiguousarray(y[SAMPLE:])[None], np.ascontiguousarray(y[:SAMPLE])[None],
            kv(r["out_k_new"]), kv(r["out_v_new"]),
            np.ascontiguousarray(r["out_ssd_new"].transpose(1, 2, 0)).reshape(1, 1, 2, HEADS_SSD, SSD_P, P),
            np.ascontiguousarray(r["out_hg_new"].transpose(1, 2, 0, 3))[None, None])
```

```python
from contextlib import ExitStack

import numpy as np
import concourse.bass as bass
from concourse import mybir

F32 = mybir.dt.float32
F32R = mybir.dt.float32r
U8 = mybir.dt.uint8
ALU = mybir.AluOpType
ACT = mybir.ActivationFunctionType
AX_X = mybir.AxisListType.X

P = 128
D_MODEL = 1024
KT = D_MODEL // P
SAMPLE, PROMPT = 512, 128
NT = SAMPLE + PROMPT
HALF = NT // 2
SEQS = ((0, SAMPLE, 1), (SAMPLE, NT, 0))
TT = NT // P
PROMPT_TT = TT - 1
EPS = 1e-6
F_FLOOR = 1e-30
HEADS_SSD, SSD_P, SSD_GROUPS = 16, 64, 2
HPG = HEADS_SSD // SSD_GROUPS
HG_HEADS, HG_SET = 8, 4
LEVELS = 7
ATTN_HEADS, KV_HEADS, HD = 16, 4, 64
FFN_T = 2816 // P
FFN_H = FFN_T // 2
RING = 4
ADA_RING = 2
N_ADA = 2 * 6 * KT
ADA_FIRST = 2 * KT
CP = NT + 1
UP = NT + 3

_SMALL = [("cond", KT * 2), ("ada_b", N_ADA), ("norm_g", 2 * 4 * KT), ("sconv_w", 3 * 12), ("sconv_b", 12),
          ("fconv_w", 2 * 3 * 44), ("fconv_b", 2 * 44), ("ssd_g", KT), ("hg_g", KT), ("ssd_d", KT),
          ("lb", 2 * KT), ("q_g", 1), ("k_g", 1), ("dt_b", 32), ("a_log", 32)]
SMALL = {}
_n = 0
for _name, _w in _SMALL:
    SMALL[_name] = (_n, _n + _w)
    _n += _w
N_SMALL = _n
IDENT, ONES, GT, LT, LE, GE, BD64, ROT = range(8)


def plan():
    tiles, slot = [], 0

    def full(kind, i):
        nonlocal slot
        tiles.append((kind, i, [(slot, k, k) for k in range(KT)]))
        slot += 1

    def ffn(layer):
        nonlocal slot
        for half in range(2):
            for i in range(FFN_H):
                full("gate", (layer, half * FFN_H + i))
                full("val", (layer, half * FFN_H + i))
            for m in range(KT):
                t = [(slot + (m * FFN_H + k) // KT, (m * FFN_H + k) % KT, k) for k in range(FFN_H)]
                tiles.append(("down", (layer, half, m), t))
            slot += FFN_H

    full("dt", 0)
    for g in range(SSD_GROUPS):
        for i in (8 + g, 10 + g, 4 * g, 4 * g + 1, 4 * g + 2, 4 * g + 3):
            full("conv", i)
        for i in range(4):
            full("z", 4 * g + i)
    for g in range(2):
        for i in range(4):
            full("q", 4 * g + i)
        for d in range(2):
            for i in range(4):
                full("zf", (d, 4 * g + i))
        for i in range(4):
            full("v", 4 * g + i)
    for i in range(KT):
        full("og", i)
    for half in (1, 0):
        for i in range(KT):
            full("out", (half, i))
    ffn(0)
    for i in range(8):
        full("aq", i)
    for i in range(4):
        full("ak", i)
    for i in range(2):
        full("av", i)
    for i in range(KT):
        full("aout", i)
    ffn(1)
    return tiles, slot


TILES, N_SLOTS = plan()
LAST_TILE = {}
for _t, (_k, _i, _kts) in enumerate(TILES):
    for _s, _, _ in _kts:
        LAST_TILE[_s] = _t
MID_SLOTS = [_s for _s in range(N_SLOTS) if TILES[LAST_TILE[_s]][2][-1][0] != _s]
MID_COUNT = {_s: _n + 1 for _n, _s in enumerate(MID_SLOTS)}
FIRST_OF = {}
for _t, (_k, _i, _kts) in enumerate(TILES):
    FIRST_OF.setdefault(_k, _t)
    FIRST_OF.setdefault((_k, _i[0] if isinstance(_i, tuple) else _i), _t)
    FIRST_OF.setdefault((_k, _i), _t)

def ada_after(t):
    a = ADA_FIRST + t
    return a if a < N_ADA else None


NORMS = [8] + [1] * 8 + [8] + [8, 8, 8, 8] + [1] * 12 + [8, 8, 8]
N_ADALN0, N_HG, N_SSD, N_RES0, N_FFN0, N_RES1, N_ATT, N_QK, N_RES2, N_FFN1, N_RES3 = 0, 1, 9, 10, 11, 12, 13, 14, 26, 27, 28
POOLED = (N_SSD, N_RES0, N_RES1, N_RES2, N_RES3)
NORM_BASE = [sum(NORMS[:i]) for i in range(len(NORMS) + 1)]

HG_PAIRS = [(PROMPT_TT, PROMPT_TT), (0, 3), (1, 2), (2, 1), (3, 0)]
SSD_STATES = [(0, PROMPT_TT), (1, PROMPT_TT), (0, 0), (1, 3), (0, 1), (1, 2), (0, 2), (1, 1)]
SSD_UNITS = [(t, q) for t in (PROMPT_TT, 0, 1, 2, 3) for q in range(2)]
ATT_UNITS = [(h, b) for h in range(ATTN_HEADS) for b in range(TT)]


def hybrid_step(nc, x, cond_small, consts, masks8, rope, s_ssd, s_hg, cache_k, cache_v, wstream, wada,
                y_out, k_out, v_out, ssd_out, hg_out):
    yssd_dram = nc.dram_tensor("yssd_scratch", [P, KT * NT], F32).ap()
    with ExitStack() as ctx:
        def sb(name, shape, dt=F32, stack=ctx):
            return stack.enter_context(nc.sbuf_tensor(name, shape, dt))

        def sem(name):
            return ctx.enter_context(nc.semaphore(name))

        ring = sb("ring", [P, RING, KT, P])
        adaring = sb("adaring", [P, ADA_RING, KT, P])
        whi = sb("whi", [P, 2, KT, P], F32R)
        wlo = sb("wlo", [P, 2, KT, P], F32R)
        hh = sb("hh", [P, KT, NT], F32R)
        hl = sb("hl", [P, KT, NT], F32R)
        ybuf = sb("ybuf", [P, KT, NT])
        sq = sb("sq", [P, 2, NT + 2])
        rt = sb("rt", [P, NT])
        rb = sb("rb", [P, NT])
        wk = sb("wk", [P, 4, NT + 4])
        cm = sb("cm", [P, 8, P])
        m8 = sb("m8", [P, 2 * LEVELS * 64 + P], U8)
        small = sb("small", [P, N_SMALL])
        mod = sb("mod", [P, N_ADA, 2])
        condT = sb("condT", [P, KT, 2])
        scal = sb("scal", [P, 6, KT, 2])
        lbt = sb("lbt", [P, 4, 2 * KT])

        def par(name, a=None, b=None):
            lo, hi = SMALL[name]
            return small[:, lo:hi] if a is None else small[:, lo + a:lo + (a + 1 if b is None else b)]

        with ExitStack() as ph:
            xsT = sb("xsT", [P, 4, NT], F32, ph)
            bcT = sb("bcT", [P, 2, NT], F32, ph)
            zs = sb("zs", [P, 4, NT], F32, ph)
            xtok = sb("xtok", [P, TT, 512], F32, ph)
            btok = sb("btok", [P, TT, P], F32, ph)
            st = sb("st", [P, 2, 4, 512], F32, ph)
            ra = sb("ra", [P, 2, 4, P], F32, ph)
            eg = sb("eg", [P, 2, 4, P], F32, ph)
            ec = sb("ec", [P, 2, 4, P], F32, ph)
            xd = sb("xd", [P, 2, 512], F32, ph)
            cbm = sb("cbm", [P, 2, P], F32, ph)
            dtt = sb("dtt", [P, TT, 32], F32, ph)
            adt = sb("adt", [P, TT, 32], F32, ph)
            dtw = sb("dtw", [P, 3, TT, 32], F32, ph)
            eal = sb("eal", [P, 32], F32, ph)
            dect = sb("dect", [P, 4, TT, HPG], F32, ph)
            wdec = sb("wdec", [P, 2, TT, HPG], F32, ph)
        with ExitStack() as ph:
            qs = sb("qs", [P, HG_SET, NT], F32, ph)
            fg = sb("fg", [P, 2, HG_SET, NT], F32, ph)
            kg = sb("kg", [P, 2, HG_SET, NT], F32, ph)
            vtok = sb("vtok", [P, TT, HG_SET * P], F32, ph)
            tp = sb("tp", [P, 2, HG_SET, P], F32, ph)
            att = sb("att", [P, 2, HG_SET, P], F32, ph)
            hst = sb("hst", [P, 2, HG_SET, P], F32, ph)
            hfin = sb("hfin", [P, 2, HG_SET, P], F32, ph)
        qp = wk[:, 0:2, 0:HG_SET * P].rearrange("p d (h t) -> p d h t", h=HG_SET)
        ktok = wk[:, 2:4, 0:HG_SET * P].rearrange("p d (h t) -> p d h t", h=HG_SET)
        mask_in = ybuf[:, 0:2].rearrange("p f t -> p (f t)")[:, 0:2 * LEVELS * 64 + P]
        sfin, xw = sq[:, 0, 0:512], sq[:, 1, 0:512]
        heads4 = lambda a: a.rearrange("p d (h t) -> p d h t", h=4)
        egs = [eg, heads4(wk[:, 2:4, 0:512])]
        ecs = [ec, heads4(sq[:, :, 0:512])]
        xds = [[xd[:, 0], xd[:, 1]], [rt[:, 0:512], rb[:, 0:512]]]
        cbms = [[cbm[:, 0], cbm[:, 1]], [rt[:, 512:NT], rb[:, 512:NT]]]
        xT = sb("xT", [P, KT, NT])
        with ExitStack() as ph:
            adabig = sb("adabig", [P, ADA_FIRST - ADA_RING, KT, P], F32, ph)
        with ExitStack() as ph:
            gh = sb("gh", [P, FFN_H, NT], F32R, ph)
            gl = sb("gl", [P, FFN_H, NT], F32R, ph)
        with ExitStack() as ph:
            aq = sb("aq", [P, 8, NT], F32, ph)
            ak = sb("ak", [P, KV_HEADS, NT + P], F32, ph)
            av = sb("av", [P, TT + 1, KV_HEADS * HD], F32, ph)
            pr = sb("pr", [P, 3, NT], F32, ph)
            pt = sb("pt", [P, 2, TT, P], F32, ph)
            cs = sb("cs", [P, 2, SAMPLE], F32, ph)
            ck = sb("ck", [P, KV_HEADS, 2, HD], F32, ph)
            kout = sb("kout", [P, KV_HEADS, HD], F32, ph)
            mxs = sb("mxs", [P, 4, 4], F32, ph)

        pg = ctx.enter_context(nc.psum_tensor("pg", [P, 2, 1024], F32))
        ps = ctx.enter_context(nc.psum_tensor("ps", [P, 4, 512], F32))
        pn = ps[:, 2:4, 0:HALF]

        def tile_of(t):
            return pg[:, t % 2].rearrange("p (h t) -> p h t", h=2)[:, :, 0:HALF]

        def two(a):
            return a.rearrange("p (h t) -> p h t", h=2)

        def state_bank(d):
            return pg[:, 1, 512:1024] if d else ps[:, 3, :]

        def pada(a):
            if a < ADA_FIRST:
                return pg[:, a // 2 % 2, a % 2 * 512:a % 2 * 512 + 2]
            return pg[:, a % 2, 1000:1002]


        small_in = sem("small_in")
        x_in = sem("x_in")
        x_again = sem("x_again")
        w_loaded = [sem(f"w_loaded{i}") for i in range(RING)]
        ada_loaded = [sem(f"ada_loaded{i}") for i in range(ADA_RING)]
        whi_ready = sem("whi_ready")
        wlo_ready = sem("wlo_ready")
        part_used = sem("part_used")
        tile_ready = sem("tile_ready")
        tile_free = [sem(f"tile_free{i}") for i in range(2)]
        cond_ready = sem("cond_ready")
        ada_ready = sem("ada_ready")
        mod_ready = sem("mod_ready")
        sq_ready = sem("sq_ready")
        nsum_ready = sem("nsum_ready")
        ac_ready = sem("ac_ready")
        yn_ready = sem("yn_ready")
        vt_ready = sem("vt_ready")
        vt_done = sem("vt_done")
        adabig_loaded = [sem(f"adabig_loaded{i}") for i in range(ADA_FIRST - ADA_RING)]
        rt_ready = sem("rt_ready")
        r_ready = sem("r_ready")
        t_ready = sem("t_ready")
        aff_ready = sem("aff_ready")
        h_ready = sem("h_ready")
        x_ready = sem("x_ready")
        conv_ready = sem("conv_ready")
        conv_done = sem("conv_done")
        g_ready = sem("g_ready")
        dt_abs = sem("dt_abs")
        dt_log = sem("dt_log")
        dt_ready = sem("dt_ready")
        tr_ready = sem("tr_ready")
        tr_done = sem("tr_done")
        s0_in = sem("s0_in")
        dsum_ready = sem("dsum_ready")
        dexp_ready = sem("dexp_ready")
        xw_ready = sem("xw_ready")
        ls_ready = sem("ls_ready")
        st_ready = sem("st_ready")
        sfin_out = sem("sfin_out")
        cb_used = sem("cb_used")
        cb_ready = sem("cb_ready")
        ra_ready = sem("ra_ready")
        dd_ready = sem("dd_ready")
        ex_ready = sem("ex_ready")
        exc_ready = sem("exc_ready")
        g_done = sem("g_done")
        cs_ready = sem("cs_ready")
        yu_ready = sem("yu_ready")
        yu_done = sem("yu_done")
        yd_ready = sem("yd_ready")
        yz_ready = sem("yz_ready")
        yssd_out = sem("yssd_out")
        yssd_in = sem("yssd_in")
        lb_d = sem("lb_d")
        lb_e = sem("lb_e")
        fk_ready = sem("fk_ready")
        att_zero = sem("att_zero")
        qp_ready = sem("qp_ready")
        dg_ready = sem("dg_ready")
        lv_ready = sem("lv_ready")
        kk_ready = sem("kk_ready")
        kt_ready = sem("kt_ready")
        kt_done = sem("kt_done")
        o_ready = sem("o_ready")
        o_done = [sem(f"o_done{i}") for i in range(2)]
        hs_ready = sem("hs_ready")
        hs_done = sem("hs_done")
        hst_in = sem("hst_in")
        hfin_out = sem("hfin_out")
        og_done = sem("og_done")
        kv_in = sem("kv_in")
        qk_norm = sem("qk_norm")
        rot_ready = sem("rot_ready")
        rope_done = sem("rope_done")
        ko_ready = sem("ko_ready")
        sc_ready = sem("sc_ready")
        mx_ready = sem("mx_ready")
        pe_exp = sem("pe_exp")
        pr_ready = sem("pr_ready")
        pt_ready = sem("pt_ready")
        pt_done = sem("pt_done")
        ao_ready = sem("ao_ready")
        ao_done = sem("ao_done")
        kv_out = sem("kv_out")
        y_written = sem("y_written")
        vch = sem("vector_chain")
        ach = sem("scalar_chain")

        block = ctx.enter_context(nc.Block())

        def modulated(eng, i):
            if i <= ADA_FIRST:
                eng.wait_ge(mod_ready, i)
            else:
                for b in range(2):
                    eng.wait_ge(tile_free[b], freed(b, i - ADA_FIRST))

        def conv_cols(a):
            return a[:, 0:SAMPLE], a[:, SAMPLE + 1:CP]

        def halves(ap, w, t):
            return ap.rearrange("p h (b t w) -> p h b t w", t=2, w=w)[:, :, :, t, :]

        def tlevel(d, i):
            off = P - (P >> (i - 1))
            return tp[:, d, :, off:off + (P >> i)]

        def mod_at(layer, part, ft, c):
            i = (layer * 6 + part) * KT + ft
            return mod[:, i, c:c + 1]

        @block.sync
        def _(sp):
            sp.dma_start(small[:], cond_small).then_inc(small_in, 16)
            sp.dma_start(cm[:], consts).then_inc(small_in, 16)
            sp.dma_start(xT[:], x).then_inc(x_in, 16)
            sp.dma_start(mask_in, masks8).then_inc(small_in, 16)

            def load_ada(a):
                if ADA_RING <= a < ADA_FIRST:
                    sp.dma_start(adabig[:, a - ADA_RING], wada[a]).then_inc(adabig_loaded[a - ADA_RING], 16)
                    return
                if a >= ADA_FIRST + ADA_RING:
                    sp.wait_ge(tile_ready, a - ADA_FIRST - ADA_RING + 1)
                elif a >= ADA_FIRST:
                    sp.wait_ge(ada_ready, a - ADA_FIRST + 1)
                sp.dma_start(adaring[:, a % ADA_RING], wada[a]).then_inc(ada_loaded[a % ADA_RING], 16)

            def load_w(s):
                if s >= RING:
                    sp.wait_ge(wlo_ready, s - RING + 1)
                sp.dma_start(ring[:, s % RING], wstream[s]).then_inc(w_loaded[s % RING], 16)

            for a in range(ADA_FIRST):
                load_ada(a)
            for s in range(RING - 1):
                load_w(s)
            at = 0
            for s in range(RING - 1, N_SLOTS):
                load_w(s)
                a = ada_after(at)
                if a is not None and LAST_TILE.get(s - 2, -1) >= at:
                    load_ada(a)
                    at += 1

        @block.tensor
        def _(pe):
            def ada(a):
                if ADA_RING <= a < ADA_FIRST:
                    pe.wait_ge(adabig_loaded[a - ADA_RING], 16)
                    w = adabig[:, a - ADA_RING]
                else:
                    turn = 0 if a < ADA_RING else (a - ADA_FIRST) // ADA_RING + 1
                    pe.wait_ge(ada_loaded[a % ADA_RING], 16 * (turn + 1))
                    w = adaring[:, a % ADA_RING]
                if 4 <= a < ADA_FIRST:
                    pe.wait_ge(mod_ready, a - 3)
                for k in range(KT):
                    last = nc.tensor.matmul(pada(a), w[:, k, :], condT[:, k, :],
                                            start=k == 0, stop=k == KT - 1)
                last.then_inc(ada_ready if a < ADA_FIRST else tile_ready, 1)

            def gemm(t, h_base=None, g_base=None, steps=None):
                kind, _, kts = TILES[t]
                out = tile_of(t)
                first, end = steps or (0, len(kts))
                if t >= 2 and first == 0:
                    pe.wait_ge(tile_free[t % 2], t // 2)
                hi, lo = (gh, gl) if kind == "down" else (hh, hl)
                seen = -1
                for n, (s, pos, k) in list(enumerate(kts))[first:end]:
                    if s > seen:
                        pe.wait_ge(wlo_ready, s + 1)
                        seen = s
                    if h_base is not None:
                        pe.wait_ge(h_ready, h_base + k + 1)
                    if g_base is not None:
                        pe.wait_ge(g_ready, g_base + k + 1)
                    for m, (a, w) in enumerate(((hi, whi), (lo, whi), (hi, wlo))):
                        for half in range(2):
                            last = nc.tensor.matmul(out[:, half], w[:, s % 2, pos, :],
                                                    a[:, k, half * HALF:(half + 1) * HALF],
                                                    start=n == 0 and m == 0, stop=n == len(kts) - 1 and m == 2)
                    if s in MID_COUNT and LAST_TILE[s] == t and kts[n + 1][0] != s:
                        last.then_inc(part_used, 1)
                if end < len(kts):
                    return
                a = ada_after(t)
                if a is not None:
                    ada(a)
                else:
                    last.then_inc(tile_ready, 1)

            def norm(n, which=ONES):
                if n >= 1:
                    pe.wait_ge(rt_ready, n)
                if n in POOLED:
                    pe.wait_ge(ac_ready, ac_count(NORM_BASE[n + 1]))
                count = 1 if n in POOLED else NORMS[n]
                for i in range(count):
                    if n in POOLED:
                        src = rt
                    else:
                        pe.wait_ge(sq_ready, NORM_BASE[n] + i + 1)
                        src = sq[:, (NORM_BASE[n] + i) % 2]
                    for half in range(2):
                        last = nc.tensor.matmul(pn[:, half], cm[:, which, :], src[:, half * HALF:(half + 1) * HALF],
                                                start=i == 0, stop=i == count - 1)
                    last.then_inc(nsum_ready, 1)

            def transposes(j, jobs):
                if j >= 2:
                    pe.wait_ge(tr_done, j - 1)
                for i, src in enumerate(jobs):
                    last = nc.tensor.transpose(ps[:, j % 2, i * P:(i + 1) * P], src, cm[:, IDENT, :])
                last.then_inc(tr_ready, 1)

            def turn(n, t, src):
                pe.wait_ge(tile_free[t % 2], t // 2 + 1)
                if n:
                    pe.wait_ge(vt_done, n)
                bank = ps[:, 0:2].rearrange("p a b -> p (a b)")
                for tt in range(TT):
                    last = nc.tensor.transpose(bank[:, tt * P:(tt + 1) * P], src[:, tt * P:(tt + 1) * P],
                                               cm[:, IDENT, :])
                last.then_inc(vt_ready, 1)

            def ssd(g, z1):
                pe.wait_ge(conv_done, 6 * (g + 1))
                pe.wait_ge(dt_ready, 1)
                j = 7 * g
                tok = lambda t: slice(t * P, (t + 1) * P)
                transposes(j, [bcT[:, 0, tok(t)] for t in range(4)])
                transposes(j + 1, [bcT[:, 0, tok(4)]])
                for t in range(TT):
                    transposes(j + 2 + t, [xsT[:, i, tok(t)] for i in range(4)])
                for d in range(2):
                    a = adt[:, :, d * 16 + HPG * g:d * 16 + HPG * (g + 1)]
                    for n, m in enumerate(((GT, LT)[d], ONES)):
                        o = (2 * d + n) * TT * HPG
                        last = nc.tensor.matmul(ps[:, 2, o:o + TT * HPG].rearrange("p (t h) -> p t h", t=TT),
                                                cm[:, m, :], a, start=True, stop=True)
                last.then_inc(dsum_ready, 1)
                for n, (d, t) in enumerate(SSD_STATES):
                    n += g * len(SSD_STATES)
                    pe.wait_ge(xw_ready, n + 1)
                    if n:
                        pe.wait_ge(st_ready, n)
                    if d == 0 and t == PROMPT_TT:
                        pe.wait_ge(tr_done, 7 * (g + 1))
                    nc.tensor.matmul(ps[:, 3, :], btok[:, t, :], xw, start=True, stop=True).then_inc(ls_ready, 1)
                    a, b = ((n % len(SSD_STATES)) * 3, (n % len(SSD_STATES) + 1) * 3)
                    while a < b:
                        c = min(b, (a // KT + 1) * KT)
                        gemm(z1 + a // KT, steps=(a % KT, a % KT + c - a))
                        a = c
                pe.wait_ge(st_ready, (g + 1) * len(SSD_STATES))
                pe.wait_ge(dexp_ready, g + 1)
                def decays(n):
                    (t, q), u = SSD_UNITS[n], g * len(SSD_UNITS) + n
                    if q == 0:
                        if u:
                            pe.wait_ge(cb_used, u // 2)
                        nc.tensor.matmul(ps[:, 2, 0:P], bcT[:, 0, tok(t)], bcT[:, 1, tok(t)],
                                         start=True, stop=True).then_inc(cb_ready, 1)
                    for d in range(2):
                        v = 2 * u + d
                        pe.wait_ge(ra_ready, v + 1)
                        if v:
                            pe.wait_ge(ex_ready, v)
                        nc.tensor.matmul(ps[:, 0, :], cm[:, (GT, LT)[d], :], ra[:, d].rearrange("p h t -> p (h t)"),
                                         start=True, stop=True).then_inc(dd_ready, 1)
                        if v:
                            pe.wait_ge(exc_ready, v)
                        nc.tensor.matmul(ps[:, 1, :], cm[:, ONES, :], ra[:, d].rearrange("p h t -> p (h t)"),
                                         start=True, stop=True).then_inc(dd_ready, 1)

                decays(0)
                for n, (t, q) in enumerate(SSD_UNITS):
                    u = g * len(SSD_UNITS) + n
                    if n + 1 < len(SSD_UNITS):
                        decays(n + 1)
                    pe.wait_ge(g_done, 2 * u + 2)
                    pe.wait_ge(cs_ready, 2 * u + 2)
                    if u:
                        pe.wait_ge(yu_done, u)
                    for h in range(4):
                        o = ps[64 * (h % 2):64 * (h % 2) + 64, 3, (h // 2) * P:(h // 2 + 1) * P]
                        hp = slice((4 * q + h) * SSD_P, (4 * q + h + 1) * SSD_P)
                        for d in range(2):
                            off = t != PROMPT_TT
                            last = nc.tensor.matmul(o, xds[u // 2 % 2][d][:, hp], egs[u % 2][:, d, h, :], start=d == 0,
                                                    stop=d == 1 and not off, skip_group_check=True)
                            if off:
                                last = nc.tensor.matmul(o, st[:, d, t, hp], ecs[u % 2][:, d, h, :], start=False,
                                                        stop=d == 1, skip_group_check=True)
                    last.then_inc(yu_ready, 1)

            def hgrn(g):
                pe.wait_ge(fk_ready, 8 * (g + 1))
                for b in range(2):
                    pe.wait_ge(tile_free[b], freed(b, FIRST_OF[("v", 4 * g)] + 4))

                def diagonals(p):
                    np_ = g * len(HG_PAIRS) + p
                    tok = [slice(t * P, (t + 1) * P) for t in HG_PAIRS[p]]
                    for d in range(2):
                        if np_:
                            pe.wait_ge(qp_ready, qp_need(np_ - 1, 0, 0))
                        for h in range(HG_SET):
                            last = nc.tensor.matmul(pg[:, 0, d * 512 + h * P:d * 512 + (h + 1) * P], kg[:, d, h, tok[d]],
                                                    qs[:, h, tok[d]], start=True, stop=True)
                        last.then_inc(dg_ready, 1)

                diagonals(0)
                for p, pair in enumerate(HG_PAIRS):
                    np_ = g * len(HG_PAIRS) + p
                    tok = [slice(t * P, (t + 1) * P) for t in pair]
                    if np_:
                        pe.wait_ge(o_done[1], np_)
                    for i in range(LEVELS):
                        for d in range(2):
                            n = (np_ * LEVELS + i) * 2 + d
                            pe.wait_ge(qp_ready, qp_need(np_, i, d))
                            if i:
                                pe.wait_ge(kk_ready, n - 1)
                            for h in range(HG_SET):
                                last = nc.tensor.matmul(ps[:, d, h * P:(h + 1) * P], kg[:, d, h, tok[d]],
                                                        qp[:, d, h, :], start=True, stop=True)
                            last.then_inc(lv_ready, 1)
                    for d in range(2):
                        v = 2 * (np_ - g) + d
                        pe.wait_ge(qp_ready, qp_need(np_, LEVELS, d))
                        if p == len(HG_PAIRS) - 1:
                            continue
                        pe.wait_ge(kk_ready, 2 * LEVELS * np_ + 2 * (LEVELS - 1) + d + 1)
                        if v >= 2:
                            pe.wait_ge(kt_done, v - 1)
                            pe.wait_ge(hs_done, v - 1)
                        for h in range(HG_SET):
                            last = nc.tensor.transpose(pg[:, 1, d * 512 + h * P:d * 512 + (h + 1) * P], kg[:, d, h, tok[d]],
                                                       cm[:, IDENT, :])
                        last.then_inc(kt_ready, 1)
                    if p < len(HG_PAIRS) - 1:
                        diagonals(p + 1)
                    for d in range(2):
                        if np_:
                            pe.wait_ge(o_done[d], np_)
                        if p == 1:
                            pe.wait_ge(hst_in, 16 * (g + 1))
                        for h in range(HG_SET):
                            o = ps[:, 2 - d, h * P:(h + 1) * P]
                            last = nc.tensor.matmul(o, vtok[:, pair[d], h * P:(h + 1) * P], att[:, d, h, :],
                                                    start=True, stop=p == 0)
                            if p:
                                last = nc.tensor.matmul(o, hst[:, d, h, :], qp[:, d, h, :], start=False, stop=True)
                        last.then_inc(o_ready, 1)
                    if p < len(HG_PAIRS) - 1:
                        for d in range(2):
                            v = 2 * (np_ - g) + d
                            pe.wait_ge(kt_done, v + 1)
                            if v >= 2:
                                pe.wait_ge(hs_done, v - 1)
                            for h in range(HG_SET):
                                last = nc.tensor.matmul(state_bank(d)[:, h * P:(h + 1) * P], ktok[:, d, h, :],
                                                        vtok[:, pair[d], h * P:(h + 1) * P], start=True, stop=True)
                            last.then_inc(hs_ready, 1)

            def ffn(layer):
                for half in range(2):
                    t0 = FIRST_OF[("gate", (layer, half * FFN_H))]
                    for i in range(2 * FFN_H):
                        gemm(t0 + i, h_base=H_BASE["ffn0" if layer == 0 else "ffn1"] if not half and not i else None)
                    for m in range(KT):
                        gemm(t0 + 2 * FFN_H + m, g_base=(2 * layer + half) * FFN_H if m == 0 else None)

            pe.wait_ge(small_in, 48)
            norm(N_ADALN0)
            pe.wait_ge(cond_ready, 1)
            for a in range(ADA_FIRST):
                ada(a)
            t = 0
            for g in range(SSD_GROUPS):
                for _ in range(8 if g == 0 else 7):
                    gemm(t, h_base=0 if t == 0 else None)
                    if t == 1:
                        turn(0, 0, sq[:, 0])
                    t += 1
                ssd(g, t)
                t += 3
            pe.wait_ge(att_zero, 1)
            pe.wait_ge(yu_done, 2 * len(SSD_UNITS))
            for g in range(2):
                for i in range(16):
                    gemm(t)
                    if i == 13 and g:
                        pe.wait_ge(o_done[1], len(HG_PAIRS))
                    if i > 12:
                        turn(4 * g + i - 12, t - 1, wk[:, (i - 13) % 2])
                    t += 1
                turn(4 * g + 4, t - 1, wk[:, 1])
                pe.wait_ge(vt_done, 4 * g + 5)
                hgrn(g)
            for h in range(KT):
                gemm(t)
                t += 1
                if h == 0:
                    for d in range(2):
                        pe.wait_ge(o_done[d], 10)
                    pe.wait_ge(hs_done, 16)
                norm(N_HG + h)
            for m in range(KT):
                gemm(t, h_base=H_BASE["hg"] if m == 0 else None)
                t += 1
                if m == KT - 3:
                    norm(N_SSD)
            for m in range(KT):
                gemm(t, h_base=H_BASE["ssd"] if m == 0 else None)
                t += 1
            norm(N_RES0)
            norm(N_FFN0)
            ffn(0)
            norm(N_RES1)
            norm(N_ATT)
            t = FIRST_OF["aq"]
            for i in range(14 + 2):
                if i < 14:
                    gemm(t + i, h_base=H_BASE["att"] if i == 0 else None)
                if 1 <= i <= 12:
                    norm(N_QK + i - 1, BD64)
                if 2 <= i <= 13:
                    j = i - 2
                    pe.wait_ge(qk_norm, j + 1)
                    if j:
                        pe.wait_ge(rope_done, j)
                    src = aq[:, j, 0:SAMPLE] if j < 8 else ak[:, j - 8, 0:SAMPLE]
                    nc.tensor.matmul(ps[:, 1, :], cm[:, ROT, :], src, start=True, stop=True).then_inc(rot_ready, 1)
            pe.wait_ge(rope_done, 12)
            for i in range(2):
                turn(9 + i, FIRST_OF["av"] + i, wk[:, 2 + i])
            pe.wait_ge(vt_done, 11)
            pe.wait_ge(kv_in, 16 * 5)
            transposes(14, [ck[:, kv].rearrange("p a b -> p (a b)") for kv in range(KV_HEADS)])
            transposes(15, [ak[:, kv, SAMPLE:NT] for kv in range(KV_HEADS)])
            pe.wait_ge(tr_done, 16)
            for b in range(2):
                pe.wait_ge(tile_free[b], freed(b, FIRST_OF["aout"]))

            def keys(b):
                if b == PROMPT_TT:
                    return [(0, P, SAMPLE)], [PROMPT_TT]
                return [(0, SAMPLE, 0), (SAMPLE, NT, NT)], [0, 1, 2, 3, 5]

            def att_scores(u):
                h, b = ATT_UNITS[u]
                kv, r = h // (ATTN_HEADS // KV_HEADS), HD * (h % 2)
                if u >= 2:
                    pe.wait_ge(pe_exp, u - 1)
                for c0, c1, k0 in keys(b)[0]:
                    last = nc.tensor.matmul(pg[:, u % 2, c0:c1], aq[r:r + HD, h // 2, b * P:(b + 1) * P],
                                            ak[r:r + HD, kv, k0:k0 + c1 - c0], start=True, stop=True)
                last.then_inc(sc_ready, 1)

            def att_out(u):
                h, b = ATT_UNITS[u]
                kv, r = h // (ATTN_HEADS // KV_HEADS), HD * (h % 2)
                vt = keys(b)[1]
                pe.wait_ge(pr_ready, u + 1)
                if u:
                    pe.wait_ge(pt_done, u)
                bank = ps[:, 0:2, :].rearrange("p a b -> p (a b)")
                for j in range(len(vt)):
                    last = nc.tensor.transpose(bank[:, j * P:(j + 1) * P], pr[:, u % 3, j * P:(j + 1) * P],
                                               cm[:, IDENT, :])
                last.then_inc(pt_ready, 1)

            def att_pv(u):
                h, b = ATT_UNITS[u]
                kv, r = h // (ATTN_HEADS // KV_HEADS), HD * (h % 2)
                vt = keys(b)[1]
                pe.wait_ge(pt_done, u + 1)
                if u >= 2:
                    pe.wait_ge(ao_done, u - 1)
                for j, v in enumerate(vt):
                    last = nc.tensor.matmul(ps[r:r + HD, 2 + u % 2, 0:P], av[:, v, kv * HD:(kv + 1) * HD],
                                            pt[:, u % 2, j, :], start=j == 0, stop=j == len(vt) - 1)
                last.then_inc(ao_ready, 1)

            nu = len(ATT_UNITS)
            for u in range(nu + 3):
                if u < nu:
                    att_scores(u)
                if 2 <= u < nu + 2:
                    att_out(u - 2)
                if u >= 3:
                    att_pv(u - 3)
            t = FIRST_OF["aout"]
            for m in range(KT):
                if m < 2:
                    pe.wait_ge(pe_exp, nu)
                gemm(t + m, h_base=H_BASE["ao"] if m == 0 else None)
            norm(N_RES2)
            norm(N_FFN1)
            ffn(1)
            norm(N_RES3)

        @block.scalar
        def _(act):
            chain = [0]
            prepped = [0]

            def link(ins):
                chain[0] += 1
                ins.then_inc(ach, 1)
                act.wait_ge(ach, chain[0])

            def prep(t):
                upto = min(TILES[t][2][-1][0] + 2, N_SLOTS)
                for s in range(prepped[0], upto):
                    act.wait_ge(w_loaded[s % RING], 16 * (s // RING + 1))
                    if s >= 2:
                        if s - 2 in MID_COUNT:
                            act.wait_ge(part_used, MID_COUNT[s - 2])
                        else:
                            act.wait_ge(tile_ready, LAST_TILE[s - 2] + 1)
                    nc.scalar.copy(whi[:, s % 2], ring[:, s % RING]).then_inc(whi_ready, 1)
                prepped[0] = max(prepped[0], upto)

            def squares(n, src, waits, width=D_MODEL, tiles=None):
                for i in tiles or range(NORMS[n]):
                    c = NORM_BASE[n] + i
                    waits(i)
                    if c >= 2:
                        m = max(m for m in range(len(NORMS)) if NORM_BASE[m] <= c - 2)
                        if m in POOLED:
                            act.wait_ge(ac_ready, ac_count(c - 1))
                        else:
                            act.wait_ge(nsum_ready, ns_count(m) + c - 1 - NORM_BASE[m])
                    nc.scalar.activation(sq[:, c % 2, 0:NT], src(i), ACT.Square,
                                         scale=float(width) ** -0.5).then_inc(sq_ready, 1)

            def root(n):
                act.wait_ge(nsum_ready, ns_count(n + 1))
                if n:
                    act.wait_ge(r_ready, n)
                nc.scalar.activation(two(rt[:]), pn, ACT.Sqrt, bias=EPS).then_inc(rt_ready, 1)

            def affine(k, layer, which, base):
                modulated(act, (layer * 6 + 3 * which + 2) * KT)
                for ft in range(KT):
                    n = k * KT + ft
                    act.wait_ge(t_ready, n + 1)
                    if ft >= 2:
                        act.wait_ge(h_ready, base + ft - 1)
                    for lo, hi, c in SEQS:
                        last = nc.scalar.activation(wk[:, 2 + ft % 2, lo:hi], wk[:, ft % 2, lo:hi], ACT.Identity,
                                                    scale=scal[:, 0, ft, c:c + 1],
                                                    bias=mod_at(layer, 3 * which, ft, c))
                    last.then_inc(aff_ready, 1)

            def arrived(t):
                act.wait_ge(tile_ready, t + 1)
                a = ada_after(t)
                if a is not None:
                    nc.scalar.activation(mod[:, a, :], pada(a), ACT.Identity, bias=par("ada_b", a))

            def conv_in(t, n):
                if n >= 2:
                    act.wait_ge(conv_ready, n - 1)
                arrived(t)
                a, b = tile_of(t)[:, 0], tile_of(t)[:, 1]
                nc.scalar.copy(wk[:, n % 2, 1:HALF + 1], a)
                nc.scalar.copy(wk[:, n % 2, HALF + 1:SAMPLE + 1], b[:, 0:SAMPLE - HALF])
                nc.scalar.copy(wk[:, n % 2, SAMPLE + 2:UP - 1], b[:, SAMPLE - HALF:]).then_inc(tile_free[t % 2], 1)

            def evac(t, dst, func=ACT.Copy, scale=1.0):
                arrived(t)
                nc.scalar.activation(two(dst), tile_of(t), func, scale=scale).then_inc(tile_free[t % 2], 1)

            def turned(n, dst):
                act.wait_ge(vt_ready, n + 1)
                bank = ps[:, 0:2].rearrange("p a b -> p (a b)")[:, 0:NT]
                nc.scalar.copy(dst, bank.rearrange("p (t n) -> p t n", t=TT)).then_inc(vt_done, 1)

            def tr_evac(j, dst, n):
                act.wait_ge(tr_ready, j + 1)
                nc.scalar.copy(dst, ps[:, j % 2, 0:n]).then_inc(tr_done, 1)

            def ssd(g, z1):
                j = 7 * g
                if g:
                    act.wait_ge(yz_ready, 1)
                for i in range(4):
                    if i == 0:
                        act.wait_ge(conv_done, 6 * (g + 1))
                    last = nc.scalar.activation(ybuf[:, 4 * g + i], xsT[:, i], ACT.Copy,
                                                scale=par("ssd_d", 4 * g + i))
                last.then_inc(yd_ready, 1)
                tr_evac(j, btok[:, 0:4].rearrange("p t n -> p (t n)"), 4 * P)
                tr_evac(j + 1, btok[:, 4], P)
                for t in range(TT):
                    tr_evac(j + 2 + t, xtok[:, t], 4 * P)
                act.wait_ge(dsum_ready, g + 1)
                nc.scalar.activation(dect[:].rearrange("p a t h -> p (a t h)"), ps[:, 2, 0:4 * TT * HPG],
                                     ACT.Exp).then_inc(dexp_ready, 1)
                for i in range(1, 4):
                    evac(z1 + i - 1, zs[:, i], ACT.Silu)
                    if i < 3:
                        prep(z1 + i)
                for n in range(len(SSD_UNITS)):
                    u = g * len(SSD_UNITS) + n
                    for d in range(2):
                        v = 2 * u + d
                        act.wait_ge(dd_ready, 2 * v + 1)
                        if n == 1 and d == 0:
                            act.wait_ge(sfin_out, 32 * (g + 1))
                            act.wait_ge(ls_ready, (g + 1) * len(SSD_STATES))
                        if u >= 2:
                            act.wait_ge(yu_ready, u - 1)
                        nc.scalar.activation(egs[u % 2][:, d], ps[:, 0, :].rearrange("p (h t) -> p h t", h=4),
                                             ACT.Exp).then_inc(ex_ready, 1)
                        act.wait_ge(dd_ready, 2 * v + 2)
                        nc.scalar.activation(ecs[u % 2][:, d], ps[:, 1, :].rearrange("p (h t) -> p h t", h=4),
                                             ACT.Exp).then_inc(exc_ready, 1)

            def hgrn(g):
                for p, pair in enumerate(HG_PAIRS):
                    np_ = g * len(HG_PAIRS) + p
                    for d in range(2 if p < len(HG_PAIRS) - 1 else 0):
                        v = 2 * (np_ - g) + d
                        act.wait_ge(kt_ready, v + 1)
                        if v >= 2:
                            act.wait_ge(hs_ready, 2 * (np_ - g))
                        nc.scalar.copy(ktok[:, d].rearrange("p h t -> p (h t)"),
                                       pg[:, 1, d * 512:(d + 1) * 512]).then_inc(kt_done, 1)
                    for d in range(2):
                        v = 2 * np_ + d
                        if not (p in (1, 2) or (p == 0 and d == 0)):
                            continue
                        if v == 0:
                            act.wait_ge(yssd_out, 32)
                        act.wait_ge(o_ready, v + 1)
                        nc.scalar.copy(ybuf[:, g * HG_SET:(g + 1) * HG_SET, pair[d] * P:(pair[d] + 1) * P],
                                       ps[:, 2 - d, :].rearrange("p (h t) -> p h t", h=HG_SET)).then_inc(o_done[d], 1)

            nt = lambda t: (tile_free[t % 2], t // 2 + 1)

            def x_squares(n, k):
                squares(n, lambda i: xT[:, i], lambda i: act.wait_ge(x_ready, KT * k + i + 1))
                root(n)

            def y_tiles(n, t0, m):
                tiles = [m - 1] if m else []
                if m == KT - 1:
                    tiles.append(m)
                if tiles:
                    squares(n, lambda i: ybuf[:, i], lambda i: act.wait_ge(*nt(t0 + i)), tiles=tiles)
                if m == KT - 1:
                    root(n)

            def ffn(layer):
                n0 = 12 + layer * 4 * FFN_H
                for half in range(2):
                    t0 = FIRST_OF[("gate", (layer, half * FFN_H))]
                    for i in range(2 * FFN_H):
                        t, n = t0 + i, n0 + half * 2 * FFN_H + i
                        prep(t)
                        conv_in(t, n)
                        if i % 2 == 0:
                            act.wait_ge(conv_ready, n + 1)
                            gi = (2 * layer + half) * FFN_H + i // 2
                            if gi:
                                act.wait_ge(g_ready, gi)
                            nc.scalar.activation(sq[:, 0, 0:CP], wk[:, 2 + n % 2, 0:CP], ACT.Silu).then_inc(conv_done, 1)
                    for m in range(KT):
                        t = t0 + 2 * FFN_H + m
                        prep(t)
                        if half == 0:
                            evac(t, ybuf[:, m])
                        else:
                            y_tiles((N_RES1, N_RES3)[layer], t - m, m)

            act.wait_ge(small_in, 48)
            nc.scalar.activation(condT[:].rearrange("p k c -> p (k c)"), par("cond"), ACT.Silu).then_inc(cond_ready, 1)
            act.wait_ge(lb_d, 1)
            nc.scalar.activation(lbt[:, 1], lbt[:, 0], ACT.Exp).then_inc(lb_e, 1)
            squares(N_ADALN0, lambda i: xT[:, i], lambda i: act.wait_ge(x_in, 16) if i == 0 else None)
            root(N_ADALN0)
            prep(0)
            affine(0, 0, 0, 0)
            t = n = 0
            for g in range(SSD_GROUPS):
                if g == 0:
                    prep(t)
                    evac(t, sq[:, 0, 0:NT])
                    prep(t + 1)
                    act.wait_ge(dt_abs, 1)
                    nc.scalar.activation(eal[:], par("a_log"), ACT.Exp)
                    link(nc.scalar.activation(dtw[:, 2], dtw[:, 1], ACT.Exp, scale=-1.0))
                    nc.scalar.activation(dtw[:, 1], dtw[:, 2], ACT.Ln, bias=1.0).then_inc(dt_log, 1)
                    t += 1
                for i in range(6):
                    prep(t)
                    if n == 6:
                        act.wait_ge(yu_done, len(SSD_UNITS))
                    conv_in(t, n)
                    act.wait_ge(conv_ready, n + 1)
                    dst = bcT[:, i] if i < 2 else xsT[:, i - 2]
                    a, b = conv_cols(wk[:, 2 + n % 2])
                    nc.scalar.activation(dst[:, 0:SAMPLE], a, ACT.Silu)
                    nc.scalar.activation(dst[:, SAMPLE:NT], b, ACT.Silu).then_inc(conv_done, 1)
                    t += 1
                    n += 1
                prep(t)
                if g:
                    act.wait_ge(yz_ready, 1)
                evac(t, zs[:, 0], ACT.Silu)
                prep(t + 1)
                ssd(g, t + 1)
                t += 4
            for g in range(2):
                if g == 0:
                    act.wait_ge(yz_ready, 2)
                    act.wait_ge(sfin_out, 64)
                for i in range(4):
                    prep(t)
                    evac(t, qs[:, i], ACT.Silu)
                    t += 1
                if g:
                    act.wait_ge(kk_ready, 2 * LEVELS * len(HG_PAIRS))
                for d in range(2):
                    for i in range(4):
                        prep(t)
                        arrived(t)
                        nc.scalar.activation(two(fg[:, d, i]), tile_of(t), ACT.Sigmoid)
                        nc.scalar.activation(two(kg[:, d, i]), tile_of(t), ACT.Sigmoid,
                                             scale=-1.0).then_inc(tile_free[t % 2], 1)
                        t += 1
                for i in range(4):
                    prep(t)
                    if i >= 2:
                        act.wait_ge(vt_ready, 4 * g + i)
                    evac(t, wk[:, i % 2, 0:NT])
                    if i:
                        turned(4 * g + i, vtok[:, :, (i - 1) * P:i * P])
                    t += 1
                turned(4 * g + 4, vtok[:, :, 3 * P:4 * P])
                hgrn(g)
            act.wait_ge(o_done[0], 10)
            act.wait_ge(o_done[1], 10)
            for h in range(KT):
                prep(t)
                squares(N_HG + h, lambda i, h=h: ybuf[:, h], lambda i: None, width=P)
                if h >= 2:
                    act.wait_ge(og_done, h - 1)
                evac(t, wk[:, h % 2, 0:NT], ACT.Silu)
                root(N_HG + h)
                t += 1
            for m in range(KT):
                prep(t)
                if m == 0:
                    act.wait_ge(h_ready, H_BASE["hg"] + KT)
                evac(t, ybuf[:, m])
                if m < 4:
                    squares(N_SSD, lambda i: xT[:, i], lambda i: act.wait_ge(yssd_in, 16) if i == 0 else None,
                            tiles=[2 * m, 2 * m + 1])
                if m == KT - 2:
                    root(N_SSD)
                t += 1

            for m in range(KT):
                prep(t)
                y_tiles(N_RES0, t - m, m)
                t += 1
            x_squares(N_FFN0, 0)
            affine(1, 0, 1, H_BASE["ffn0"])
            ffn(0)
            x_squares(N_ATT, 1)
            affine(2, 1, 0, H_BASE["att"])
            t0 = FIRST_OF["aq"]
            for i in range(14):
                t = t0 + i
                prep(t)
                if i < 12:
                    dst = aq[:, i] if i < 8 else ak[:, i - 8, 0:NT]
                    evac(t, dst)
                    squares(N_QK + i, lambda _, dst=dst: dst, lambda _, t=t: act.wait_ge(*nt(t)), width=HD)
                else:
                    evac(t, wk[:, 2 + i - 12, 0:NT])
                if 1 <= i <= 12:
                    root(N_QK + i - 1)
            for i in range(2):
                turned(9 + i, av[:, 0:TT, i * P:(i + 1) * P])
            tr_evac_k = (ak[:, :, NT:NT + P], kout[:])
            act.wait_ge(tr_ready, 15)
            nc.scalar.copy(tr_evac_k[0], ps[:, 0, :].rearrange("p (k t) -> p k t", k=KV_HEADS)).then_inc(tr_done, 1)
            act.wait_ge(tr_ready, 16)
            nc.scalar.copy(tr_evac_k[1], ps[:, 1, :].rearrange("p (k t) -> p k t", k=KV_HEADS)[:, :, 0:HD]).then_inc(tr_done, 1)
            prep(FIRST_OF["aout"] - 1)
            nu = len(ATT_UNITS)

            def att_exp(u):
                n = P if ATT_UNITS[u][1] == PROMPT_TT else NT
                act.wait_ge(mx_ready, u + 1)
                if u >= 3:
                    act.wait_ge(pt_ready, u - 2)
                nc.scalar.activation(pr[:, u % 3, 0:n], pg[:, u % 2, 0:n], ACT.Exp, scale=HD ** -0.5,
                                     bias=mxs[:, u % 4, 1:2], accum_out=mxs[:, u % 4, 2:3]).then_inc(pe_exp, 1)

            def att_pt(u):
                n = P if ATT_UNITS[u][1] == PROMPT_TT else NT
                act.wait_ge(pt_ready, u + 1)
                if u >= 2:
                    act.wait_ge(ao_ready, u - 1)
                nc.scalar.copy(pt[:, u % 2].rearrange("p t n -> p (t n)")[:, 0:n],
                               ps[:, 0:2, :].rearrange("p a b -> p (a b)")[:, 0:n]).then_inc(pt_done, 1)

            for u in range(nu + 2):
                if u >= 2:
                    att_pt(u - 2)
                if u < nu:
                    att_exp(u)
            for m in range(KT):
                prep(FIRST_OF["aout"] + m)
                y_tiles(N_RES2, FIRST_OF["aout"], m)
            x_squares(N_FFN1, 2)
            affine(3, 1, 1, H_BASE["ffn1"])
            ffn(1)
            for ft in range(KT):
                act.wait_ge(x_ready, 3 * KT + ft + 1)
                act.dma_start(y_out[:, ft], xT[:, ft]).then_inc(y_written, 16)
            act.wait_ge(y_written, 16 * KT)

        @block.vector
        def _(dve):
            chain = [0]
            prepped = [0]
            V = nc.vector

            def link(ins):
                chain[0] += 1
                ins.then_inc(vch, 1)
                dve.wait_ge(vch, chain[0])

            def prep(t):
                upto = min(TILES[t][2][-1][0] + 2, N_SLOTS)
                for s in range(prepped[0], upto):
                    dve.wait_ge(whi_ready, s + 1)
                    V.tensor_tensor(wlo[:, s % 2], ring[:, s % RING], whi[:, s % 2].bitcast(F32),
                                    ALU.subtract).then_inc(wlo_ready, 1)
                prepped[0] = max(prepped[0], upto)

            def arrived(t):
                dve.wait_ge(tile_ready, t + 1)
                a = ada_after(t)
                if a is not None:
                    V.tensor_scalar(mod[:, a, :], pada(a), par("ada_b", a), None, ALU.add)

            def ada(a):
                dve.wait_ge(ada_ready, a + 1)
                V.tensor_scalar(mod[:, a, :], pada(a), par("ada_b", a), None, ALU.add).then_inc(mod_ready, 1)

            def recip(n):
                dve.wait_ge(rt_ready, n + 1)
                V.reciprocal(rb[:], rt[:]).then_inc(r_ready, 1)
                dve.wait_ge(r_ready, n + 1)

            def split(dst, src, n):
                link(V.tensor_copy(dst[0], src))
                V.tensor_tensor(dst[1], src, dst[0].bitcast(F32), ALU.subtract).then_inc(h_ready, 1)

            def adaln(k, layer, which, base, n):
                modulated(dve, (layer * 6 + 3 * which + 2) * KT)
                i = (layer * 6 + 3 * which + 1) * KT
                gcol = (layer * 4 + 2 * which) * KT
                g = par("norm_g", gcol, gcol + KT).unsqueeze(2).broadcast_to([P, KT, 2])
                link(V.scalar_tensor_tensor(out=scal[:, 0], in0=mod[:, i:i + KT, :], scalar=1.0, in1=g,
                                            op0=ALU.add, op1=ALU.mult))
                if n != N_ADALN0:
                    recip(n)
                for ft in range(KT + 1):
                    if ft < KT:
                        if ft >= 2:
                            dve.wait_ge(aff_ready, k * KT + ft - 1)
                        V.tensor_tensor(wk[:, ft % 2, 0:NT], xT[:, ft], rb[:], ALU.mult).then_inc(t_ready, 1)
                    if ft:
                        f = ft - 1
                        dve.wait_ge(aff_ready, k * KT + f + 1)
                        split((hh[:, f], hl[:, f]), wk[:, 2 + f % 2, 0:NT], base + f)

            def residual(k, layer, which, n):
                i = (layer * 6 + 3 * which + 2) * KT
                modulated(dve, i + KT)
                gcol = (layer * 4 + 2 * which + 1) * KT
                g = par("norm_g", gcol, gcol + KT).unsqueeze(2).broadcast_to([P, KT, 2])
                link(V.tensor_tensor(scal[:, 1], mod[:, i:i + KT, :], g, ALU.mult))
                recip(n)
                if k == 0:
                    dve.wait_ge(x_again, 16)
                for ft in range(KT):
                    if ft in POOL_TILES:
                        dve.wait_ge(yn_ready, k * len(POOL_TILES) + POOL_TILES.index(ft) + 1)
                    else:
                        link(V.tensor_tensor(ybuf[:, ft], ybuf[:, ft], rb[:], ALU.mult))
                    for lo, hi, c in SEQS:
                        last = V.scalar_tensor_tensor(out=xT[:, ft, lo:hi], in0=ybuf[:, ft, lo:hi],
                                                      scalar=scal[:, 1, ft, c:c + 1], in1=xT[:, ft, lo:hi],
                                                      op0=ALU.mult, op1=ALU.add)
                    last.then_inc(x_ready, 1)

            def pads():
                for c in (0, SAMPLE + 1, UP - 1):
                    last = V.memset(wk[:, 0:2, c:c + 1], 0.0)
                link(last)

            def conv(t, n, w, b):
                dve.wait_ge(tile_free[t % 2], t // 2 + 1)
                u, c = wk[:, n % 2], wk[:, 2 + n % 2, 0:CP]
                link(V.tensor_scalar(c, u[:, 1:CP + 1], w[1], b, ALU.mult, ALU.add))
                link(V.scalar_tensor_tensor(out=c, in0=u[:, 0:CP], scalar=w[0], in1=c, op0=ALU.mult, op1=ALU.add))
                ins = V.scalar_tensor_tensor(out=c, in0=u[:, 2:CP + 2], scalar=w[2], in1=c, op0=ALU.mult, op1=ALU.add)
                ins.then_inc(conv_ready, 1)

            def per_head(a, n):
                return a.unsqueeze(2).broadcast_to([P, a.shape[1], n])

            def ssd(g, z1):
                ns = len(SSD_STATES)
                hs = lambda d: slice(d * 16 + HPG * g, d * 16 + HPG * (g + 1))
                dve.wait_ge(dexp_ready, g + 1)
                for d in range(2):
                    last = V.tensor_tensor(wdec[:, d], dtt[:, :, hs(d)], dect[:, 2 * d], ALU.mult)
                link(last)
                dve.wait_ge(tr_done, 7 * (g + 1))
                dve.wait_ge(s0_in, 16 * 2 * (g + 1))
                for i, (d, t) in enumerate(SSD_STATES):
                    n = g * ns + i
                    if i in (4, 7):
                        prep(z1 + (1 if i == 4 else 2))
                    if n:
                        dve.wait_ge(ls_ready, n)
                    V.tensor_tensor(xw.rearrange("p (h n) -> p h n", h=HPG),
                                    xtok[:, t].rearrange("p (h n) -> p h n", h=HPG),
                                    per_head(wdec[:, d, t], SSD_P), ALU.mult).then_inc(xw_ready, 1)
                    if t == PROMPT_TT:
                        dve.wait_ge(ls_ready, n + 1)
                        if 2 * g + d:
                            dve.wait_ge(sfin_out, 16 * (2 * g + d))
                        V.tensor_copy(sfin, ps[:, 3, :]).then_inc(st_ready, 1)
                        continue
                    nxt = t + 1 if d == 0 else t - 1
                    view = lambda a: a.rearrange("p (h n) -> p h n", h=HPG)
                    link(V.tensor_tensor(view(st[:, d, nxt]), view(st[:, d, t]),
                                         per_head(dect[:, 2 * d + 1, t], SSD_P), ALU.mult))
                    dve.wait_ge(ls_ready, n + 1)
                    V.tensor_tensor(st[:, d, nxt], st[:, d, nxt], ps[:, 3, :], ALU.add).then_inc(st_ready, 1)
                    dve.wait_ge(st_ready, n + 1)
                dve.wait_ge(yd_ready, g + 1)
                def step_sizes(n, d):
                    (t, q), u = SSD_UNITS[n], g * len(SSD_UNITS) + n
                    if u:
                        dve.wait_ge(dd_ready, 4 * (u - 1) + 2 * d + 2)
                    a = adt[:, t, d * 16 + HPG * g + 4 * q:d * 16 + HPG * g + 4 * q + 4]
                    V.tensor_tensor(ra[:, d], per_head(a, P),
                                    cm[:, (LE, GE)[d], :].unsqueeze(1).broadcast_to([P, 4, P]),
                                    ALU.mult).then_inc(ra_ready, 1)

                def add_output(n):
                    (t, q), u = SSD_UNITS[n], g * len(SSD_UNITS) + n
                    dve.wait_ge(yu_ready, u + 1)
                    y = ybuf[:, 4 * g + 2 * q:4 * g + 2 * q + 2, t * P:(t + 1) * P]
                    V.tensor_tensor(y, y, ps[:, 3, 0:2 * P].rearrange("p (f t) -> p f t", f=2),
                                    ALU.add).then_inc(yu_done, 1)

                nu = len(SSD_UNITS)
                for d in range(2):
                    step_sizes(0, d)
                for i, (t, q) in enumerate(SSD_UNITS):
                    u = g * nu + i
                    if q == 0:
                        dve.wait_ge(cb_ready, u // 2 + 1)
                        if u >= 4:
                            dve.wait_ge(yu_ready, u - 2)
                        for d in range(2):
                            last = V.tensor_tensor(cbms[u // 2 % 2][d], ps[:, 2, 0:P], cm[:, (LE, GE)[d], :], ALU.mult)
                        last.then_inc(cb_used, 1)
                        dve.wait_ge(cb_used, u // 2 + 1)
                        for d in range(2):
                            last = V.tensor_tensor(xds[u // 2 % 2][d].rearrange("p (h n) -> p h n", h=HPG),
                                                   xtok[:, t].rearrange("p (h n) -> p h n", h=HPG),
                                                   per_head(dtt[:, t, hs(d)], SSD_P), ALU.mult)
                    for d in range(2):
                        dve.wait_ge(ex_ready, 2 * u + d + 1)
                        V.tensor_tensor(egs[u % 2][:, d], egs[u % 2][:, d],
                                        cbms[u // 2 % 2][d].unsqueeze(1).broadcast_to([P, 4, P]),
                                        ALU.mult).then_inc(g_done, 1)
                        if i + 1 < nu:
                            step_sizes(i + 1, d)
                    if i:
                        add_output(i - 1)
                add_output(nu - 1)
                for b in range(2):
                    dve.wait_ge(tile_free[b], freed(b, z1 + 3))
                dve.wait_ge(yu_done, (g + 1) * len(SSD_UNITS))
                V.tensor_tensor(ybuf[:, 4 * g:4 * g + 4], ybuf[:, 4 * g:4 * g + 4], zs[:], ALU.mult).then_inc(yz_ready, 1)

            def hgrn(g):
                def start(p):
                    np_ = g * len(HG_PAIRS) + p
                    for d in range(2):
                        tok = slice(HG_PAIRS[p][d] * P, (HG_PAIRS[p][d] + 1) * P)
                        if np_:
                            dve.wait_ge(o_ready, 2 * np_ - 1 + d)
                        V.tensor_tensor(qp[:, d], qs[:, :, tok], fg[:, d, :, tok], ALU.mult).then_inc(qp_ready, 1)
                        dve.wait_ge(dg_ready, 2 * np_ + d + 1)
                        V.copy_predicated(att[:, d], m8[:, 2 * LEVELS * 64:].unsqueeze(1).broadcast_to([P, HG_SET, P]),
                                          pg[:, 0, d * 512:(d + 1) * 512]
                                          .rearrange("p (h t) -> p h t", h=HG_SET)).then_inc(qp_ready, 1)

                start(0)
                for p, pair in enumerate(HG_PAIRS):
                    np_ = g * len(HG_PAIRS) + p
                    tok = [slice(t * P, (t + 1) * P) for t in pair]
                    for i in range(LEVELS):
                        w = 1 << i
                        for d in range(2):
                            n = (np_ * LEVELS + i) * 2 + d
                            dve.wait_ge(lv_ready, n + 1)
                            mo = (d * LEVELS + i) * 64
                            mask = m8[:, mo:mo + 64].rearrange("p (b w) -> p b w", w=w).unsqueeze(1)
                            V.copy_predicated(halves(att[:, d], w, 1 - d), mask.broadcast_to([P, HG_SET, 64 // w, w]),
                                              halves(ps[:, d].rearrange("p (h t) -> p h t", h=HG_SET), w, 1 - d))
                            tot = fg[:, d, :, tok[d]] if i == 0 else tlevel(d, i)
                            pairs = tot.rearrange("p h (b t) -> p h b t", t=2)
                            V.tensor_tensor(tlevel(d, i + 1), pairs[:, :, :, 0], pairs[:, :, :, 1], ALU.mult)
                            q = halves(qp[:, d], w, 1 - d)
                            V.tensor_tensor(q, q, pairs[:, :, :, d].unsqueeze(3)
                                            .broadcast_to([P, HG_SET, 64 // w, w]), ALU.mult).then_inc(qp_ready, 1)
                    for d in range(2):
                        v = 2 * np_ + d
                        if d == 1 and p < len(HG_PAIRS) - 1:
                            start(p + 1)
                        if p in (1, 2) or (p == 0 and d == 0):
                            continue
                        dve.wait_ge(o_ready, v + 1)
                        dve.wait_ge(o_done[0], np_ if d == 0 else np_ + 1) if (d or np_) else None
                        dve.wait_ge(o_done[1], np_) if np_ else None
                        o = ybuf[:, g * HG_SET:(g + 1) * HG_SET, tok[d]]
                        V.tensor_tensor(o, o, ps[:, 2 - d, :].rearrange("p (h t) -> p h t", h=HG_SET),
                                        ALU.add).then_inc(o_done[d], 1)
                    if p < len(HG_PAIRS) - 1:
                        for d in range(2):
                            v = 2 * (np_ - g) + d
                            dve.wait_ge(hs_ready, v + 1)
                            src = state_bank(d).rearrange("p (h t) -> p h t", h=HG_SET)
                            if p == 0:
                                if g:
                                    dve.wait_ge(hfin_out, 32)
                                V.tensor_copy(hfin[:, d], src).then_inc(hs_done, 1)
                                continue
                            dve.wait_ge(hst_in, 16 * (g + 1))
                            for h in range(HG_SET):
                                last = V.scalar_tensor_tensor(out=hst[:, d, h], in0=hst[:, d, h],
                                                              scalar=tlevel(d, LEVELS)[:, h], in1=src[:, h],
                                                              op0=ALU.mult, op1=ALU.add)
                            last.then_inc(hs_done, 1)

            def ffn(layer):
                n0 = 12 + layer * 4 * FFN_H
                fw = lambda tap, i: par("fconv_w", (layer * 3 + tap) * 44 + i)
                pads()
                if layer:
                    dve.wait_ge(kv_out, 32)
                for half in range(2):
                    t0 = FIRST_OF[("gate", (layer, half * FFN_H))]
                    for i in range(2 * FFN_H):
                        t, n = t0 + i, n0 + half * 2 * FFN_H + i
                        prep(t)
                        feat = half * FFN_H + i // 2 + (i % 2) * FFN_T
                        conv(t, n, [fw(k, feat) for k in range(3)], par("fconv_b", layer * 44 + feat))
                        if i % 2:
                            gi = i // 2
                            gn = (2 * layer + half) * FFN_H + gi
                            dve.wait_ge(conv_ready, n + 1)
                            dve.wait_ge(conv_done, 12 + gn + 1)
                            if half and gi == 0:
                                dve.wait_ge(tile_ready, t0)
                            for lo, hi, c in SEQS:
                                o = 1 - c
                                last = V.tensor_tensor(sq[:, 1, lo:hi], wk[:, 2 + n % 2, lo + o:hi + o],
                                                       sq[:, 0, lo + o:hi + o], ALU.mult)
                            link(last)
                            link(V.tensor_copy(gh[:, gi], sq[:, 1, 0:NT]))
                            V.tensor_tensor(gl[:, gi], sq[:, 1, 0:NT], gh[:, gi].bitcast(F32),
                                            ALU.subtract).then_inc(g_ready, 1)
                    for m in range(KT):
                        t = t0 + 2 * FFN_H + m
                        prep(t)
                        if half:
                            arrived(t)
                            V.tensor_tensor(two(ybuf[:, m]), two(ybuf[:, m]), tile_of(t),
                                            ALU.add).then_inc(tile_free[t % 2], 1)

            dve.wait_ge(small_in, 48)
            link(V.tensor_copy(m8[:], mask_in))
            V.tensor_tensor(lbt[:, 0], par("lb"), par("lb"), ALU.subtract).then_inc(lb_d, 1)
            dve.wait_ge(lb_e, 1)
            link(V.reciprocal(lbt[:, 2], lbt[:, 1]))
            link(V.tensor_tensor(lbt[:, 3], lbt[:, 1], lbt[:, 2], ALU.mult))
            link(V.tensor_tensor(lbt[:, 0], lbt[:, 3], lbt[:, 3], ALU.subtract))
            link(V.tensor_scalar(lbt[:, 1], lbt[:, 0], -1.0, 1.0, ALU.mult, ALU.add))
            recip(N_ADALN0)
            for a in range(ADA_FIRST):
                ada(a)
            prep(0)
            adaln(0, 0, 0, 0, N_ADALN0)
            pads()
            t = n = 0
            for g in range(SSD_GROUPS):
                if g == 0:
                    prep(t)
                    prep(t + 1)
                    dve.wait_ge(vt_ready, 1)
                    raw = ps[:, 0:2].rearrange("p a b -> p (a b)")[:, 0:NT].rearrange("p (t n) -> p t n", t=TT)
                    V.tensor_tensor(dtw[:, 0], raw[:, :, 0:32], par("dt_b").unsqueeze(1).broadcast_to([P, TT, 32]),
                                    ALU.add).then_inc(vt_done, 1)
                    dve.wait_ge(vt_done, 1)
                    V.scalar_tensor_tensor(out=dtw[:, 1], in0=dtw[:, 0], scalar=-1.0, in1=dtw[:, 0],
                                           op0=ALU.mult, op1=ALU.max).then_inc(dt_abs, 1)
                    dve.wait_ge(dt_log, 1)
                    link(V.scalar_tensor_tensor(out=dtt[:], in0=dtw[:, 0], scalar=0.0, in1=dtw[:, 1],
                                                op0=ALU.max, op1=ALU.add))
                    V.scalar_tensor_tensor(out=adt[:], in0=dtt[:], scalar=-1.0,
                                           in1=eal[:].unsqueeze(1).broadcast_to([P, TT, 32]),
                                           op0=ALU.mult, op1=ALU.mult).then_inc(dt_ready, 1)
                    dve.wait_ge(dt_ready, 1)
                    t += 1
                for i in range(6):
                    prep(t)
                    feat = TILES[t][1]
                    if n >= 2:
                        dve.wait_ge(conv_done, n - 1)
                    conv(t, n, [par("sconv_w", k * 12 + feat) for k in range(3)], par("sconv_b", feat))
                    t += 1
                    n += 1
                prep(t)
                prep(t + 1)
                ssd(g, t + 1)
                t += 4
            dve.wait_ge(sfin_out, 64)
            dve.wait_ge(yz_ready, 2)
            V.memset(att[:], 0.0).then_inc(att_zero, 1)
            dve.wait_ge(att_zero, 1)
            for g in range(2):
                for i in range(4):
                    prep(t)
                    t += 1
                for d in range(2):
                    for i in range(4):
                        prep(t)
                        dve.wait_ge(tile_free[t % 2], t // 2 + 1)
                        c = d * KT + g * HG_SET + i
                        link(V.tensor_scalar(fg[:, d, i], fg[:, d, i], lbt[:, 1, c:c + 1], lbt[:, 0, c:c + 1],
                                             ALU.mult, ALU.add))
                        V.tensor_scalar(fg[:, d, i], fg[:, d, i], F_FLOOR, None, ALU.max)
                        V.tensor_scalar(kg[:, d, i], kg[:, d, i], lbt[:, 1, c:c + 1], None,
                                        ALU.mult).then_inc(fk_ready, 1)
                        t += 1
                for i in range(4):
                    prep(t)
                    t += 1
                dve.wait_ge(fk_ready, 8 * (g + 1))
                dve.wait_ge(vt_ready, 4 * g + 5)
                hgrn(g)
            for h in range(KT):
                prep(t)
                recip(N_HG + h)
                dve.wait_ge(tile_free[t % 2], t // 2 + 1)
                link(V.tensor_tensor(ybuf[:, h], ybuf[:, h], rb[:], ALU.mult))
                V.scalar_tensor_tensor(out=ybuf[:, h], in0=ybuf[:, h], scalar=par("hg_g", h), in1=wk[:, h % 2, 0:NT],
                                       op0=ALU.mult, op1=ALU.mult).then_inc(og_done, 1)
                t += 1
            dve.wait_ge(tile_ready, t)
            dve.wait_ge(og_done, KT)
            for f in range(KT):
                split((hh[:, f], hl[:, f]), ybuf[:, f], H_BASE["hg"] + f)
            for m in range(KT):
                prep(t)
                t += 1
            recip(N_SSD)
            for f in range(KT):
                last = V.scalar_tensor_tensor(out=xT[:, f], in0=xT[:, f], scalar=par("ssd_g", f), in1=rb[:],
                                              op0=ALU.mult, op1=ALU.mult)
            link(last)
            dve.wait_ge(tile_ready, t)
            for f in range(KT):
                split((hh[:, f], hl[:, f]), xT[:, f], H_BASE["ssd"] + f)
            for m in range(KT):
                prep(t)
                arrived(t)
                if m == 0:
                    for b in range(2):
                        dve.wait_ge(tile_free[b], freed(b, t))
                V.tensor_tensor(two(ybuf[:, m]), two(ybuf[:, m]), tile_of(t), ALU.add).then_inc(tile_free[t % 2], 1)
                t += 1
            for b in range(2):
                dve.wait_ge(tile_free[b], freed(b, t))
            residual(0, 0, 0, N_RES0)
            adaln(1, 0, 1, H_BASE["ffn0"], N_FFN0)
            ffn(0)
            for b in range(2):
                dve.wait_ge(tile_free[b], freed(b, FIRST_OF["aq"]))
            residual(1, 0, 1, N_RES1)
            adaln(2, 1, 0, H_BASE["att"], N_ATT)
            t0 = FIRST_OF["aq"]

            def qk_finish(j):
                buf = aq[:, j] if j < 8 else ak[:, j - 8, 0:NT]
                recip(N_QK + j)
                link(V.tensor_tensor(buf, buf, rb[:], ALU.mult))
                V.tensor_scalar(buf, buf, par("q_g") if j < 8 else par("k_g"), None, ALU.mult).then_inc(qk_norm, 1)

            def rope_apply(j):
                buf = aq[:, j, 0:SAMPLE] if j < 8 else ak[:, j - 8, 0:SAMPLE]
                dve.wait_ge(rot_ready, j + 1)
                if j == 0:
                    dve.wait_ge(kv_in, 16 * 5)
                V.tensor_tensor(wk[:, 0, 0:SAMPLE], ps[:, 1, :], cs[:, 1], ALU.mult)
                link(V.tensor_tensor(buf, buf, cs[:, 0], ALU.mult))
                V.tensor_tensor(buf, buf, wk[:, 0, 0:SAMPLE], ALU.add).then_inc(rope_done, 1)

            for i in range(14):
                prep(t0 + i)
                if 1 <= i <= 12:
                    qk_finish(i - 1)
                if i >= 2:
                    rope_apply(i - 2)
            dve.wait_ge(tr_done, 16)
            prep(FIRST_OF["aout"] - 1)
            nu = len(ATT_UNITS)

            def att_max(u):
                n = P if ATT_UNITS[u][1] == PROMPT_TT else NT
                dve.wait_ge(sc_ready, u + 1)
                link(V.reduce_max(mxs[:, u % 4, 0:1], pg[:, u % 2, 0:n], AX_X))
                V.tensor_scalar(mxs[:, u % 4, 1:2], mxs[:, u % 4, 0:1], -HD ** -0.5, None, ALU.mult).then_inc(mx_ready, 1)

            def att_prob(u):
                n = P if ATT_UNITS[u][1] == PROMPT_TT else NT
                dve.wait_ge(pe_exp, u + 1)
                link(V.reciprocal(mxs[:, u % 4, 3:4], mxs[:, u % 4, 2:3]))
                V.tensor_scalar(pr[:, u % 3, 0:n], pr[:, u % 3, 0:n], mxs[:, u % 4, 3:4], None,
                                ALU.mult).then_inc(pr_ready, 1)

            def att_evac(u):
                h, b = ATT_UNITS[u]
                r = HD * (h % 2)
                dve.wait_ge(ao_ready, u + 1)
                V.tensor_copy(ybuf[r:r + HD, h // 2, b * P:(b + 1) * P],
                              ps[r:r + HD, 2 + u % 2, 0:P]).then_inc(ao_done, 1)

            for u in range(nu + 4):
                if 1 <= u <= nu:
                    att_prob(u - 1)
                if u < nu:
                    att_max(u)
                if u >= 4:
                    att_evac(u - 4)
            dve.wait_ge(ao_done, nu)
            for f in range(KT):
                split((hh[:, f], hl[:, f]), ybuf[:, f], H_BASE["ao"] + f)
            for m in range(KT):
                t = FIRST_OF["aout"] + m
                prep(t)
                dve.wait_ge(tile_ready, t + 1)
                if m == 0:
                    dve.wait_ge(h_ready, H_BASE["ao"] + KT)
                V.tensor_copy(two(ybuf[:, m]), tile_of(t)).then_inc(tile_free[t % 2], 1)
            t = FIRST_OF["aout"] + KT
            for b in range(2):
                dve.wait_ge(tile_free[b], freed(b, t))
            residual(2, 1, 0, N_RES2)
            adaln(3, 1, 1, H_BASE["ffn1"], N_FFN1)
            ffn(1)
            for b in range(2):
                dve.wait_ge(tile_free[b], freed(b, len(TILES)))
            residual(3, 1, 1, N_RES3)

        @block.gpsimd
        def _(pool):
            G = nc.gpsimd

            def add_squares(n):
                if n:
                    pool.wait_ge(r_ready, n)
                for i in range(NORMS[n]):
                    c = NORM_BASE[n] + i
                    k = ac_count(c)
                    pool.wait_ge(sq_ready, c + 1)
                    if i == 0:
                        G.tensor_copy(rt[:], sq[:, c % 2, 0:NT]).then_inc(ac_ready, 1)
                    else:
                        pool.wait_ge(ac_ready, k)
                        G.tensor_tensor(rt[:], rt[:], sq[:, c % 2, 0:NT], ALU.add).then_inc(ac_ready, 1)

            def normalise(n):
                pool.wait_ge(r_ready, n + 1)
                for ft in POOL_TILES:
                    G.tensor_tensor(ybuf[:, ft], ybuf[:, ft], rb[:], ALU.mult).then_inc(yn_ready, 1)

            for g in range(SSD_GROUPS):
                if g:
                    pool.wait_ge(yu_done, len(SSD_UNITS))
                else:
                    pool.wait_ge(h_ready, KT)
                for d in range(2):
                    G.dma_start(st[:, d, 0 if d == 0 else 3], s_ssd[:, d, 512 * g:512 * (g + 1)]).then_inc(s0_in, 16)
                for d in range(2):
                    pool.wait_ge(st_ready, g * len(SSD_STATES) + d + 1)
                    G.dma_start(ssd_out[:, d, 512 * g:512 * (g + 1)], sfin).then_inc(sfin_out, 16)
                for i, (t, q) in enumerate(SSD_UNITS):
                    u = g * len(SSD_UNITS) + i
                    for d in range(2):
                        pool.wait_ge(exc_ready, 2 * u + d + 1)
                        G.tensor_tensor(ecs[u % 2][:, d], ecs[u % 2][:, d],
                                        bcT[:, 1, t * P:(t + 1) * P].unsqueeze(1).broadcast_to([P, 4, P]),
                                        ALU.mult).then_inc(cs_ready, 1)
                pool.wait_ge(yz_ready, g + 1)
                G.dma_start(yssd_dram[:, 4 * NT * g:4 * NT * (g + 1)].rearrange("p (f t) -> p f t", f=4),
                            ybuf[:, 4 * g:4 * g + 4]).then_inc(yssd_out, 16)
            pool.wait_ge(sfin_out, 64)
            for g in range(2):
                if g:
                    pool.wait_ge(o_ready, 10)
                    pool.wait_ge(hs_done, 8)
                G.dma_start(hst[:], s_hg[:, :, g * HG_SET:(g + 1) * HG_SET]).then_inc(hst_in, 16)
                for p, pair in enumerate(HG_PAIRS):
                    np_ = g * len(HG_PAIRS) + p
                    for i in range(LEVELS):
                        w = 1 << i
                        for d in range(2):
                            n = (np_ * LEVELS + i) * 2 + d
                            tok = slice(pair[d] * P, (pair[d] + 1) * P)
                            pool.wait_ge(lv_ready, n + 1)
                            tot = fg[:, d, :, tok] if i == 0 else tlevel(d, i)
                            tot = tot.rearrange("p h (b t) -> p h b t", t=2)[:, :, :, 1 - d]
                            k = halves(kg[:, d, :, tok], w, d)
                            G.tensor_tensor(k, k, tot.unsqueeze(3).broadcast_to([P, HG_SET, 64 // w, w]),
                                            ALU.mult).then_inc(kk_ready, 1)
                    if p == 0:
                        pool.wait_ge(hs_done, 8 * g + 2)
                        for d in range(2):
                            G.dma_start(hg_out[:, d, g * HG_SET:(g + 1) * HG_SET], hfin[:, d]).then_inc(hfin_out, 16)
            pool.wait_ge(o_done[0], 10)
            pool.wait_ge(o_done[1], 10)
            pool.wait_ge(hs_done, 16)
            pool.wait_ge(kk_ready, 4 * LEVELS * len(HG_PAIRS))
            pool.wait_ge(hfin_out, 64)
            pool.wait_ge(yssd_out, 32)
            G.dma_start(xT[:].rearrange("p f t -> p (f t)"), yssd_dram).then_inc(yssd_in, 16)
            add_squares(N_SSD)
            pool.wait_ge(h_ready, H_BASE["ssd"] + KT)
            G.dma_start(xT[:], x).then_inc(x_again, 16)
            for a in (N_RES0, N_RES1):
                add_squares(a)
                normalise(a)
            pool.wait_ge(tile_ready, FIRST_OF["aq"])
            for a in range(2):
                G.dma_start(ck[:, :, a], cache_k).then_inc(kv_in, 16)
            G.dma_start(av[:, TT].rearrange("p (k n) -> p k n", k=KV_HEADS), cache_v).then_inc(kv_in, 16)
            G.dma_start(cs[:, 0], rope[:, 0]).then_inc(kv_in, 16)
            G.dma_start(cs[:, 1], rope[:, 1]).then_inc(kv_in, 16)
            pool.wait_ge(tr_done, 16)
            G.dma_start(k_out, kout[:]).then_inc(kv_out, 16)
            for b in range(2):
                pool.wait_ge(tile_free[b], freed(b, FIRST_OF["aout"]))
            G.dma_start(v_out, av[:, PROMPT_TT].rearrange("p (k n) -> p k n", k=KV_HEADS)).then_inc(kv_out, 16)
            add_squares(N_RES2)
            normalise(N_RES2)
            add_squares(N_RES3)
            normalise(N_RES3)
            pool.wait_ge(kv_out, 32)


H_BASE = {"adaln0": 0, "hg": 8, "ssd": 16, "ffn0": 24, "att": 32, "ao": 40, "ffn1": 48}


POOL_TILES = (1, 2, 4, 5, 7)


def ac_count(c):
    return sum(min(max(c - NORM_BASE[m], 0), 8) for m in POOLED)


def ns_count(n):
    return sum(1 if m in POOLED else NORMS[m] for m in range(n))


def freed(b, t):
    return (t + 1 - b) // 2


def qp_need(np_, i, d):
    base = np_ * (4 + 2 * LEVELS)
    return base + 4 if i == 0 else base + 4 + 2 * (i - 1) + d + 1


def constant_arrays():
    j, s = np.arange(P)[:, None], np.arange(P)[None, :]
    rot = np.zeros((P, P), np.float32)
    for m in range(P):
        if m % 32 < 16:
            rot[m + 16, m] = -1.0
        else:
            rot[m - 16, m] = 1.0
    mats = [j == s, j >= 0 * s, j > s, j < s, j <= s, j >= s, j // 64 == s // 64]
    cm = np.stack([a.astype(np.float32) for a in mats] + [rot], axis=1)
    m8 = []
    t = np.arange(P)
    for d in range(2):
        for i in range(LEVELS):
            w = 1 << i
            late = t.reshape(-1, 2, w)[:, 1 - d].reshape(-1)
            same = (t[:, None] // (2 * w)) == (late[None, :] // (2 * w))
            other = (t[:, None] // w) % 2 == d
            m8.append(same & other)
    m8.append(j == s)
    m8 = np.concatenate(m8, axis=1).astype(np.float32)
    nf = HD // 4
    inv = np.float32(10000.0) ** (-np.arange(nf, dtype=np.float32) / np.float32(nf))
    tok = np.arange(SAMPLE)
    pos = np.stack([tok // 64, tok % 64]).astype(np.float32)
    p = np.arange(P) % HD
    ang = (pos[p // 32] * inv[p % 16][:, None]).astype(np.float32)
    rope = np.stack([np.cos(ang), np.sin(ang)], axis=1).astype(np.float32)
    return np.ascontiguousarray(cm), np.ascontiguousarray(m8), np.ascontiguousarray(rope)


def feat(a):
    a = np.asarray(a)
    return a.reshape(-1, P).T


def wtiles(w):
    return w.reshape(KT, P, -1, P).transpose(2, 1, 0, 3)


def kernel(**inputs):
    import concourse.bacc as bacc
    from concourse.bass_utils import run_bass_kernel_spmd

    v = {k: np.asarray(a) for k, a in inputs.items()}
    cm, m8, rope = constant_arrays()

    def rows(a):
        return np.broadcast_to(a.reshape(1, -1), (P, a.size))

    cond = np.stack([v["c_ctx"].reshape(KT, P).T, v["c"].reshape(KT, P).T], axis=2).reshape(P, -1)
    small = np.concatenate([
        cond, feat(v["ada_b"]), feat(v["norm_g"]), feat(v["ssd_conv_w"]), feat(v["ssd_conv_b"]),
        feat(v["ffn_conv_w"]), feat(v["ffn_conv_b"]), feat(v["ssd_norm_g"]), feat(v["hg_norm_g"]),
        feat(np.repeat(v["ssd_d"].reshape(-1), SSD_P)), feat(v["hg_lb_logits"]),
        feat(np.tile(v["attn_q_norm"].reshape(-1), 2)), feat(np.tile(v["attn_k_norm"].reshape(-1), 2)),
        rows(v["ssd_dt_bias"]), rows(v["ssd_a_log"])], axis=1)

    w_in = v["ssm_w_in"][0]
    z0, x0, dt0 = 0, 1024, 2560
    q0, f0, v0, o0 = 2592, 3616, 5664, 6688
    w_out = v["ssm_w_out"][0]
    w_qkv = v["attn_w_qkv"][0]

    def w_of(kind, i):
        col = lambda a, n: a[:, n:n + P]
        if kind == "dt":
            return np.concatenate([w_in[:, dt0:dt0 + 32], np.zeros((D_MODEL, P - 32), np.float32)], axis=1)
        if kind in ("conv", "z", "q", "v", "og"):
            return col(w_in, {"conv": x0, "z": z0, "q": q0, "v": v0, "og": o0}[kind] + P * i)
        if kind == "zf":
            return col(w_in, f0 + D_MODEL * i[0] + P * i[1])
        if kind == "out":
            return col(w_out[D_MODEL * i[0]:D_MODEL * (i[0] + 1)], P * i[1])
        if kind in ("gate", "val"):
            return col(v["ffn_w_up"][i[0]], P * (i[1] + (FFN_T if kind == "val" else 0)))
        if kind == "aq":
            return col(w_qkv, P * i)
        if kind == "ak":
            k = w_qkv[:, D_MODEL + HD * i:D_MODEL + HD * (i + 1)]
            return np.concatenate([k, k], axis=1)
        if kind == "av":
            return col(w_qkv, D_MODEL + KV_HEADS * HD + P * i)
        return col(v["attn_w_out"][0], P * i)

    stream = np.zeros((N_SLOTS, P, KT, P), np.float32)
    for kind, i, kts in TILES:
        if kind == "down":
            w = v["ffn_w_down"][i[0]][i[1] * FFN_H * P:(i[1] + 1) * FFN_H * P, P * i[2]:P * (i[2] + 1)]
            for s, pos, k in kts:
                stream[s, :, pos] = w[k * P:(k + 1) * P]
        else:
            stream[kts[0][0]] = wtiles(w_of(kind, i))[0]
    wada = np.concatenate([wtiles(v["ada_w"][0]), wtiles(v["ada_w"][1])])

    tokens = np.concatenate([v["x_sample"][0], v["x_prompt"][0]], axis=0)
    arrays = {
        "x": tokens.T.reshape(KT, P, NT).transpose(1, 0, 2),
        "small_params": small,
        "consts": cm,
        "masks8": m8,
        "rope": rope,
        "s_ssd": v["state_ssd"][0, 0].reshape(2, D_MODEL, P).transpose(2, 0, 1),
        "s_hg": v["state_hgrn"][0, 0].transpose(2, 0, 1, 3),
        "ck_in": v["cache_k"][0, 0].transpose(1, 0, 2),
        "cv_in": v["cache_v"][0, 0].transpose(1, 0, 2),
        "wstream": stream,
        "wada": wada,
    }
    outs = {"y": (P, KT, NT), "k_new": (P, KV_HEADS, HD), "v_new": (P, KV_HEADS, HD),
            "ssd_new": (P, 2, D_MODEL), "hg_new": (P, 2, HG_HEADS, P)}
    nc = bacc.Bacc("TRN2", target_bir_lowering=False, num_devices=1)
    args, data = [], {}
    for name, a in arrays.items():
        a = np.ascontiguousarray(a)
        data[f"in_{name}"] = a
        args.append(nc.dram_tensor(f"in_{name}", a.shape, mybir.dt.from_np(a.dtype), kind="ExternalInput").ap())
    for name, shape in outs.items():
        args.append(nc.dram_tensor(f"out_{name}", shape, F32, kind="ExternalOutput").ap())
    hybrid_step(nc, *args)
    r = run_bass_kernel_spmd(nc, [data], core_ids=[0]).results[0]
    y = r["out_y"].transpose(1, 0, 2).reshape(D_MODEL, NT).T
    kv = lambda a: np.ascontiguousarray(a.transpose(1, 0, 2))[None, None]
    return (np.ascontiguousarray(y[SAMPLE:])[None], np.ascontiguousarray(y[:SAMPLE])[None],
            kv(r["out_k_new"]), kv(r["out_v_new"]),
            np.ascontiguousarray(r["out_ssd_new"].transpose(1, 2, 0)).reshape(1, 1, 2, HEADS_SSD, SSD_P, P),
            np.ascontiguousarray(r["out_hg_new"].transpose(1, 2, 0, 3))[None, None])
```
